# Optimizing a Trainium2 kernel written in Bass

```python
import jax
import jax.numpy as jnp
from jax import lax
import numpy as np

D_MODEL = 1024
BATCH = 1
SEQ = 512
DEPTH = 2

CHUNK = 64
EPS = 1e-6
M_HEADS = 4
M_QK_DIM = 64
M_V_DIM = 128
M_QK_W = M_HEADS * M_QK_DIM
M_V_W = M_HEADS * M_V_DIM
M_CONV = 4
GATE_SOFTCAP = 15.0
I_GATE_BIAS = -2.0
F_GATE_BIAS = 3.0
A_Q_HEADS = 8
A_KV_HEADS = 2
A_HEAD_DIM = 64
A_Q_W = A_Q_HEADS * A_HEAD_DIM
A_KV_W = A_KV_HEADS * A_HEAD_DIM
WINDOW = 128
WINDOW_CHUNKS = WINDOW // CHUNK
ROT_DIM = A_HEAD_DIM // 4
ROPE_THETA = 500000.0
D_FF = 4 * D_MODEL
SPLITS = (2 * M_QK_W, M_V_W, M_HEADS, M_HEADS, M_V_W, A_Q_W, A_KV_W, A_KV_W, D_MODEL, D_MODEL)
D_IN = 2 * M_QK_W + 2 * M_V_W + 2 * M_HEADS + A_Q_W + 2 * A_KV_W + 2 * D_MODEL
MAX_STREAM_CHUNKS = 1024

kernel_name = 'hybrid_mlstm_swa_stream_block'

def split_cols(t):
    parts = []
    start = 0
    for size in SPLITS:
        parts.append(t[..., start:start + size])
        start += size
    return parts

def rmsnorm(x, g):
    xf = x.astype(jnp.float32)
    inv = lax.rsqrt(jnp.mean(xf * xf, axis=-1, keepdims=True) + EPS)
    return (xf * inv * g.astype(jnp.float32)).astype(x.dtype)

def softcap(t):
    return GATE_SOFTCAP * jnp.tanh(t / GATE_SOFTCAP)

def causal_depthwise_conv(x, w):
    c = x.shape[-1]
    return lax.conv_general_dilated(
        x, w[:, None, :].astype(x.dtype), window_strides=(1,),
        padding=[(M_CONV - 1, 0)], dimension_numbers=('NWC', 'WIO', 'NWC'),
        feature_group_count=c)

def rope_tables(positions):
    inv_freq = ROPE_THETA ** (-jnp.arange(0, ROT_DIM, 2, dtype=jnp.float32) / ROT_DIM)
    ang = positions.astype(jnp.float32)[..., None] * inv_freq
    return jnp.cos(ang)[:, :, None, :], jnp.sin(ang)[:, :, None, :]

def partial_rope(t, cos, sin):
    half = ROT_DIM // 2
    tf = t.astype(jnp.float32)
    t1 = tf[..., :half]
    t2 = tf[..., half:ROT_DIM]
    out = jnp.concatenate([t1 * cos - t2 * sin, t2 * cos + t1 * sin, tf[..., ROT_DIM:]], axis=-1)
    return out.astype(t.dtype)

def mlstm_chunkwise(q, k, v, log_i, log_f):
    b, s, h, dk = q.shape
    dv = v.shape[-1]
    nc = s // CHUNK
    f32 = jnp.float32

    def chunks(t):
        return t.astype(f32).reshape(b, nc, CHUNK, h, -1).transpose(1, 0, 3, 2, 4)

    def gate_chunks(t):
        return t.astype(f32).reshape(b, nc, CHUNK, h).transpose(1, 0, 3, 2)

    qc = chunks(q) * (dk ** -0.5)
    kc = chunks(k)
    vc = chunks(v)
    lic = gate_chunks(log_i)
    lfc = gate_chunks(log_f)
    causal = jnp.tril(jnp.ones((CHUNK, CHUNK), dtype=bool))

    def step(carry, inp):
        c_mat, n_vec, m_prev = carry
        qt, kt, vt, li, lf = inp
        bcum = jnp.cumsum(lf, axis=-1)
        dmat = jnp.where(causal, bcum[..., :, None] - bcum[..., None, :] + li[..., None, :], -jnp.inf)
        inter = bcum + m_prev[..., None]
        m_t = jnp.maximum(inter, jnp.max(dmat, axis=-1))
        scores = jnp.einsum('bhtd,bhsd->bhts', qt, kt) * jnp.exp(dmat - m_t[..., None])
        inter_w = jnp.exp(inter - m_t)
        num = (jnp.einsum('bhts,bhsv->bhtv', scores, vt)
               + inter_w[..., None] * jnp.einsum('bhvd,bhtd->bhtv', c_mat, qt))
        den = jnp.sum(scores, axis=-1) + inter_w * jnp.einsum('bhd,bhtd->bht', n_vec, qt)
        h_t = num / jnp.maximum(jnp.abs(den), jnp.exp(-m_t))[..., None]
        b_last = bcum[..., -1]
        g = b_last[..., None] - bcum + li
        m_new = jnp.maximum(b_last + m_prev, jnp.max(g, axis=-1))
        carry_w = jnp.exp(b_last + m_prev - m_new)
        wg = jnp.exp(g - m_new[..., None])
        c_new = carry_w[..., None, None] * c_mat + jnp.einsum('bhs,bhsv,bhsd->bhvd', wg, vt, kt)
        n_new = carry_w[..., None] * n_vec + jnp.einsum('bhs,bhsd->bhd', wg, kt)
        return (c_new, n_new, m_new), h_t

    init = (jnp.zeros((b, h, dv, dk), f32), jnp.zeros((b, h, dk), f32), jnp.zeros((b, h), f32))
    _, hs = lax.scan(step, init, (qc, kc, vc, lic, lfc))
    return hs.transpose(1, 0, 3, 2, 4).reshape(b, s, h, dv).astype(v.dtype)

def band_keys(t):
    parts = []
    for j in reversed(range(WINDOW_CHUNKS)):
        if j == 0:
            parts.append(t)
        else:
            parts.append(jnp.concatenate([jnp.zeros_like(t[:, :j]), t[:, :-j]], axis=1))
    return jnp.concatenate(parts, axis=2)

def sliding_window_attention(q, k, v, sinks):
    b, s, hq, dh = q.shape
    hkv = k.shape[2]
    grp = hq // hkv
    nc = s // CHUNK
    wl = WINDOW_CHUNKS * CHUNK
    qc = q.reshape(b, nc, CHUNK, hkv, grp, dh)
    kb = band_keys(k.reshape(b, nc, CHUNK, hkv, dh))
    vb = band_keys(v.reshape(b, nc, CHUNK, hkv, dh))
    logits = jnp.einsum('bclkgd,bcmkd->bkgclm', qc, kb).astype(jnp.float32) * (dh ** -0.5)
    key_chunk = (jnp.arange(nc)[:, None, None] - (WINDOW_CHUNKS - 1)
                 + (jnp.arange(wl) // CHUNK)[None, None, :])
    logits = jnp.where(key_chunk >= 0, logits, -jnp.inf)
    sink = sinks.astype(jnp.float32).reshape(hkv, grp)[None, :, :, None, None, None]
    sink_col = jnp.broadcast_to(sink, logits.shape[:-1] + (1,))
    probs = jax.nn.softmax(jnp.concatenate([logits, sink_col], axis=-1), axis=-1)[..., :-1]
    out = jnp.einsum('bkgclm,bcmkd->bclkgd', probs.astype(v.dtype), vb)
    return out.reshape(b, s, hq * dh)

def hybrid_mixer(h, w_in, conv_qk_w, mlstm_gate_b, mlstm_norm_g, attn_sinks,
                 w_branch_m, w_branch_a, w_out, cos, sin):
    b, s, _ = h.shape
    proj = h @ w_in
    qk_pre, v_m, i_pre, f_pre, o_pre, q_a, k_a, v_a, g_m, g_a = split_cols(proj)
    qk = jax.nn.silu(causal_depthwise_conv(qk_pre, conv_qk_w))
    q_m = qk[..., :M_QK_W].reshape(b, s, M_HEADS, M_QK_DIM)
    k_m = qk[..., M_QK_W:].reshape(b, s, M_HEADS, M_QK_DIM)
    log_i = softcap(i_pre.astype(jnp.float32) + mlstm_gate_b[:M_HEADS].astype(jnp.float32))
    log_f = jax.nn.log_sigmoid(softcap(f_pre.astype(jnp.float32) + mlstm_gate_b[M_HEADS:].astype(jnp.float32)))
    h_m = mlstm_chunkwise(q_m, k_m, v_m.reshape(b, s, M_HEADS, M_V_DIM), log_i, log_f)
    h_m = rmsnorm(h_m, mlstm_norm_g.reshape(M_HEADS, M_V_DIM)).reshape(b, s, M_V_W) * jax.nn.sigmoid(o_pre)
    q_a = partial_rope(q_a.reshape(b, s, A_Q_HEADS, A_HEAD_DIM), cos, sin)
    k_a = partial_rope(k_a.reshape(b, s, A_KV_HEADS, A_HEAD_DIM), cos, sin)
    h_a = sliding_window_attention(q_a, k_a, v_a.reshape(b, s, A_KV_HEADS, A_HEAD_DIM), attn_sinks)
    merged = jax.nn.sigmoid(g_m) * (h_m @ w_branch_m) + jax.nn.sigmoid(g_a) * (h_a @ w_branch_a)
    return merged @ w_out

def squared_relu_mlp(h, w_up, w_down):
    return jnp.square(jax.nn.relu(h @ w_up)) @ w_down

def setup_inputs(seed: int = 0) -> dict:
    key = jax.random.key(seed)
    ks = jax.random.split(key, 16)
    f32 = jnp.float32

    def nrm(k, shape, scale):
        return jax.random.normal(k, shape, f32) * scale

    x = jax.random.normal(ks[0], (BATCH, SEQ, D_MODEL), f32)
    offsets = jax.random.randint(ks[1], (BATCH, 1), 0, MAX_STREAM_CHUNKS) * CHUNK
    positions = (offsets + jnp.arange(SEQ, dtype=jnp.int32)[None, :]).astype(jnp.int32)
    gate_base = jnp.concatenate([jnp.full((M_HEADS,), I_GATE_BIAS, f32), jnp.full((M_HEADS,), F_GATE_BIAS, f32)])
    return {
        'x': x,
        'positions': positions,
        'norm_mix_g': 1.0 + nrm(ks[2], (DEPTH, D_MODEL), 0.05),
        'w_in': nrm(ks[3], (DEPTH, D_MODEL, D_IN), D_MODEL ** -0.5),
        'conv_qk_w': nrm(ks[4], (DEPTH, M_CONV, 2 * M_QK_W), M_CONV ** -0.5),
        'mlstm_gate_b': gate_base[None, :] + nrm(ks[5], (DEPTH, 2 * M_HEADS), 0.1),
        'mlstm_norm_g': 1.0 + nrm(ks[6], (DEPTH, M_V_W), 0.05),
        'attn_sinks': nrm(ks[7], (DEPTH, A_Q_HEADS), 0.5),
        'w_branch_m': nrm(ks[8], (DEPTH, M_V_W, D_MODEL), M_V_W ** -0.5),
        'w_branch_a': nrm(ks[9], (DEPTH, A_Q_W, D_MODEL), A_Q_W ** -0.5),
        'w_out': nrm(ks[10], (DEPTH, D_MODEL, D_MODEL), D_MODEL ** -0.5),
        'norm_mlp_g': 1.0 + nrm(ks[11], (DEPTH, D_MODEL), 0.05),
        'w_up': nrm(ks[12], (DEPTH, D_MODEL, D_FF), D_MODEL ** -0.5),
        'w_down': nrm(ks[13], (DEPTH, D_FF, D_MODEL), D_FF ** -0.5),
        'final_norm_g': 1.0 + nrm(ks[14], (D_MODEL,), 0.05),
    }

def reference(x, positions, norm_mix_g, w_in, conv_qk_w, mlstm_gate_b, mlstm_norm_g,
              attn_sinks, w_branch_m, w_branch_a, w_out, norm_mlp_g, w_up, w_down,
              final_norm_g):
    cos, sin = rope_tables(positions)
    for layer in range(DEPTH):
        h = rmsnorm(x, norm_mix_g[layer])
        x = x + hybrid_mixer(h, w_in[layer], conv_qk_w[layer], mlstm_gate_b[layer],
                             mlstm_norm_g[layer], attn_sinks[layer], w_branch_m[layer],
                             w_branch_a[layer], w_out[layer], cos, sin)
        h = rmsnorm(x, norm_mlp_g[layer])
        x = x + squared_relu_mlp(h, w_up[layer], w_down[layer])
    return rmsnorm(x, final_norm_g)


_drawn_inputs = setup_inputs


def setup_inputs(seed=0):
    import zlib

    import numpy as np

    out = dict(_drawn_inputs(seed))
    spreads = {}
    factors = {'mlstm_norm_g': 2.797, 'attn_sinks': 44.14}
    for name, (base, spread) in spreads.items():
        noise = np.random.default_rng([zlib.crc32(name.encode()), seed]).standard_normal(out[name].shape)
        drawn = base * np.exp(spread * noise) if base else spread * noise
        out[name] = jnp.asarray(drawn.astype(out[name].dtype))
    for name, factor in factors.items():
        out[name] = (out[name] * factor).astype(out[name].dtype)
    return out
```

```python
from contextlib import ExitStack

import concourse.bass as bass
from concourse import mybir

F32 = mybir.dt.float32
F32R = mybir.dt.float32r
I32 = mybir.dt.int32
ALU = mybir.AluOpType
ACT = mybir.ActivationFunctionType
AX = mybir.AxisListType

P = 128
SEQ, D_MODEL, DEPTH = 512, 1024, 2
KT = D_MODEL // P
TB = SEQ // P
CHUNK = 64
NC = SEQ // CHUNK
M_HEADS, M_QK, M_V, TAPS = 4, 64, 128, 4
A_HEADS, A_KV, A_DIM = 8, 2, 64
PAIRS_H = A_HEADS // 2
F_TILES = 4 * D_MODEL // P
QUARTERS = F_TILES // KT
EPS = 1e-6
CAP = 15.0
MASKED = -1e30
ROT_DIM, ROPE_THETA = A_DIM // 4, 500000.0

W_ORDER = (["qa"] * 4 + ["ka", "va"] + ["qk"] * 4 + ["vm"] * 4 + ["if", "none"] + ["gm"] * 6
           + ["o"] * 2 + ["gm"] * 2 + ["o"] * 2 + ["ga"] * 8)
W_UNITS = [(kind, W_ORDER[:n].count(kind), n) for n, kind in enumerate(W_ORDER) if kind != "none"]
NONE_POS = W_ORDER.index("none")
BRANCH_POS = len(W_ORDER)
OUT_POS = BRANCH_POS + KT
MLP_POS = OUT_POS + KT
UNITS = MLP_POS + 2 * F_TILES
PAIRS = UNITS // 2
HALVES = 2 * UNITS
F_ROW = 32

PC_CONV, PC_MLP_G, PC_NEXT_G, PC_HEAD_G, PC_GATE_B, PC_SINK = 0, 16, 24, 32, 36, 37
PCOLS = 41
C_ID, C_ROPE, C_FREQ, C_HALFPI, C_MASK, C_SEL = 0, 128, 256, 257, 258, 386
CKEPT = 258
CCOLS = 898

ATT0 = 10
MEM0 = 20
SEG = [0, 512, 896, 1152, 1280]


def bank_uses(pos):
    return pos // 2 + 1 - (1 if pos % 2 == NONE_POS % 2 and pos > NONE_POS else 0)


def program(nc, xt, pos_in, consts, params, g_first, wstream, out):
    with ExitStack() as ctx:
        layer_sems = []

        def sem(name):
            return ctx.enter_context(nc.semaphore(name))

        def lsem(name):
            s = sem(name)
            layer_sems.append(s)
            return s

        def sb(name, shape, dt=F32, where=ctx):
            return where.enter_context(nc.sbuf_tensor(name, shape, dt))

        x = sb("x", [P, KT, SEQ])
        xg_mix = sb("xg_mix", [P, KT, 2, SEQ], F32R)
        with ExitStack() as early:
            th_gate = sb("th_gate", [P, 2 * KT, SEQ], F32, early)
        xg_mlp = sb("xg_mlp", [P, KT, 2, SEQ], F32R)
        with ExitStack() as early:
            sb("skip_ha", [P, KT // 2, 2, SEQ], F32, early)
            qa = sb("qa", [P, PAIRS_H, SEQ], F32, early)
            kd = sb("kd", [P, A_KV, SEQ], F32, early)
            vwin = sb("vwin", [P, NC, P], F32, early)
        hid = sb("hid", [P, KT, 2, SEQ], F32R)
        raw = sb("raw", [P, 2, KT, 2 * P])
        whi = sb("whi", [P, 4, KT // 2, P], F32R)
        wlo = sb("wlo", [P, 4, KT // 2, P], F32R)
        cst = sb("cst", [P, CKEPT])
        par = sb("par", [P, PCOLS])
        g0 = sb("g0", [P, KT])
        ident_r = sb("ident_r", [P, P], F32R)
        mask_r = sb("mask_r", [P, P], F32R)
        sel_r = sb("sel_r", [2 * F_ROW, M_HEADS, P], F32R)
        ones = sb("ones", [P, SEQ])
        cos = sb("cos", [P, SEQ])
        sin = sb("sin", [P, SEQ])
        invb = sb("invb", [P, SEQ])
        ssum = sb("ssum", [P, SEQ])
        za = sb("za", [P, 2, SEQ])
        qk = sb("qk", [P, 4, SEQ])
        vn = sb("vn", [P, M_HEADS, TB, M_V + 1])
        frows = sb("frows", [2 * F_ROW, SEG[-1]], F32R)
        with ExitStack() as early:
            rows = sb("rows", [2 * F_ROW, 2, SEQ], F32, early)
        hn = sb("hn", [P, TB, M_V + 1])
        sb("rows_rest", [P, 2 * SEQ - TB * (M_V + 1)])
        bcols = sb("bcols", [P, TB * M_HEADS])
        turns = sb("turns", [P, SEG[-1]])
        conv_in = turns[:, 0:TAPS - 1 + SEQ]
        frow = turns[0:M_HEADS]
        th_o = turns[:, 0:2 * SEQ].rearrange("p (a t) -> p a t", a=2)
        t0 = sb("t0", [P, SEQ])
        t1 = sb("t1", [P, SEQ])
        t2 = sb("t2", [P, SEQ])
        t3 = sb("t3", [P, SEQ])
        pmat = sb("pmat", [P, 2, SEQ])
        small = sb("small", [P, 16, TB])
        smalli = sb("smalli", [P, TB], I32)
        sq_t = t3
        pos_i = t0[:].bitcast(I32)
        ident = cst[:, C_ID:C_ID + P]

        def ps(name):
            return ctx.enter_context(nc.psum_tensor(name, [P, 512], F32))

        acc = [ps("acc0"), ps("acc1")]
        b_lg = ps("b_lg")
        b_pt = ps("b_pt")
        b_av = ps("b_av")
        b_ms = ps("b_ms")
        b_nm = ps("b_nm")
        b_tr = ps("b_tr")
        mem_banks = [b_ms, b_nm]
        branch_banks = [b_lg, b_pt]

        raw_in = [sem("raw_in0"), sem("raw_in1")]
        hi_done = sem("hi_done")
        lo_done = sem("lo_done")
        half_used = sem("half_used")
        par_in = sem("par_in")
        loaded = sem("loaded")
        setup = sem("setup")
        stored = sem("stored")
        layer_go = sem("layer_go")
        at_rest = sem("at_rest")
        dve_step = lsem("dve_step")
        act_step = lsem("act_step")
        evacuated = [lsem("evacuated0"), lsem("evacuated1")]
        stat_sum, stat_diag, stat_bcast, stat_done = lsem("stat_sum"), lsem("stat_diag"), lsem("stat_bcast"), lsem("stat_done")
        partner_ready, partner_read, roped = lsem("partner_ready"), lsem("partner_read"), lsem("roped")
        vwin_t, vwin_done = lsem("vwin_t"), lsem("vwin_done")
        silu_th, qk_done = lsem("silu_th"), lsem("qk_done")
        conv_out = lsem("conv_out")
        v_t, v_done = lsem("v_t"), lsem("v_done")
        gate_th, gate_sp = lsem("gate_th"), lsem("gate_sp")
        rows_done, cols_t, cols_done = lsem("rows_done"), lsem("cols_t"), lsem("cols_done")
        logits, logits_read, att_exp, probs, probs_t, probs_c, att_o, att_hi, att_lo = (
            lsem(n) for n in ("logits", "logits_read", "att_exp", "probs", "probs_t", "probs_c", "att_o", "att_hi", "att_lo"))
        sink_gap = lsem("sink_gap")
        decay_in, scores_in, decay, weights, summed = (
            lsem(n) for n in ("decay_in", "scores_in", "decay", "weights", "summed"))
        sums_out, head_norm, head_t, head_gated, head_hi, head_lo = (
            lsem(n) for n in ("sums_out", "head_norm", "head_t", "head_gated", "head_hi", "head_lo"))
        gate_done, par_scaled = lsem("gate_done"), lsem("par_scaled")
        second_read, merged, merged_hi, merged_lo = (lsem(n) for n in ("second_read", "merged", "merged_hi", "merged_lo"))
        x_new, sq_done, sq_sum, xg_hi, xg_lo = (lsem(n) for n in ("x_new", "sq_done", "sq_sum", "xg_hi", "xg_lo"))
        relu_sq, hid_hi, hid_lo, down_scaled = (lsem(n) for n in ("relu_sq", "hid_hi", "hid_lo", "down_scaled"))
        final_out = lsem("final_out")

        block = ctx.enter_context(nc.Block())

        def unit_done(lay, pos):
            return lay * HALVES + 2 * (pos + 1) + 4

        def head_part(h):
            return (h % 2) * 64

        @block.sync
        def _(sp):
            sp.dma_start(cst[:], consts[:, 0:CKEPT]).then_inc(loaded, 16)
            sp.dma_start(pmat[:, 0, 0:P], consts[:, C_MASK:C_MASK + P]).then_inc(loaded, 16)
            sp.dma_start(pmat[0:2 * F_ROW, 1], consts[0:2 * F_ROW, C_SEL:C_SEL + M_HEADS * P]).then_inc(loaded, 16)
            sp.dma_start(g0[:], g_first).then_inc(loaded, 16)
            sp.dma_start(pos_i, pos_in.broadcast_to([P, SEQ])).then_inc(loaded, 16)
            sp.dma_start(x[:], xt.rearrange("(k p) t -> p k t", p=P)).then_inc(loaded, 16)
            for s in range(2):
                sp.dma_start(raw[:, s], wstream[s]).then_inc(raw_in[s], 16)
            with sp.Fori(0, DEPTH * PAIRS // 2 - 1) as n:
                for s in range(2):
                    sp.wait_ge(lo_done, n * 8 + 4 * (s + 1))
                    sp.dma_start(raw[:, s], wstream[2:].rearrange("(n s) p k c -> n s p k c", s=2)[n, s]).then_inc(raw_in[s], 16)
            for m in range(KT):
                sp.wait_ge(final_out, m + 1)
                sp.dma_start(out[m * P:(m + 1) * P, :], x[:, m, :]).then_inc(stored, 16)
            sp.wait_ge(stored, 16 * KT)

        @block.gpsimd
        def _(pool):
            with pool.Fori(0, DEPTH * PAIRS // 2) as n:
                for s in range(2):
                    for h in range(4):
                        pool.wait_ge(hi_done, n * 8 + (4 * s + h + 1))
                        src = raw[:, s, (h % 2) * 4:(h % 2) * 4 + 4, (h // 2) * P:(h // 2 + 1) * P]
                        nc.gpsimd.tensor_tensor(wlo[:, h], src, whi[:, h].bitcast(F32), ALU.subtract).then_inc(lo_done, 1)

        @block.scalar
        def _(act):
            steps = [0]

            def link(ins):
                steps[0] += 1
                ins.then_inc(act_step, 1)
                act.wait_ge(act_step, steps[0])

            def split_half(lay, pos, i):
                if isinstance(lay, tuple):
                    l, q = lay
                    act.wait_ge(raw_in[(pos // 2) % 2], l * (8 * PAIRS) + q * (8 * KT) + 16 * (pos // 4 + 1))
                    act.wait_ge(half_used, l * HALVES + q * (4 * KT) + (2 * pos + i + 1))
                else:
                    act.wait_ge(raw_in[(pos // 2) % 2], lay * (8 * PAIRS) + 16 * (pos // 4 + 1))
                    act.wait_ge(half_used, lay * HALVES + (2 * pos + i + 1))
                src = raw[:, (pos // 2) % 2, 4 * i:4 * i + 4, (pos % 2) * P:(pos % 2 + 1) * P]
                nc.scalar.copy(whi[:, (2 * pos + i) % 4], src).then_inc(hi_done, 1)

            act.wait_ge(setup, 1)
            nc.scalar.activation(sin[:], t1[:], ACT.Sin).then_inc(setup, 1)
            nc.scalar.activation(cos[:], t2[:], ACT.Sin, bias=cst[:, C_HALFPI:C_HALFPI + 1], scale=-1.0).then_inc(setup, 1)
            act.wait_ge(loaded, 96)
            for m in range(KT):
                nc.scalar.activation(xg_mix[:, m, 0], x[:, m], ACT.Copy, scale=g0[:, m:m + 1]).then_inc(setup, 1)
                if m:
                    act.wait_ge(sq_sum, m)
                nc.scalar.activation(sq_t[:], x[:, m], ACT.Square).then_inc(sq_done, 1)
            act.wait_ge(sq_done, KT)
            act.drain().then_inc(at_rest, 1)

            with act.Fori(0, DEPTH) as l:
                steps[0] = 0
                act.wait_ge(layer_go, l + 1)
                act.nop(nofuse=True)
                act.dma_start(par[:], params[l]).then_inc(par_in, 16)
                for pos in range(2):
                    for i in range(2):
                        split_half(l, pos, i)

                def evacuation(w):
                    kind, j, pos = W_UNITS[w]
                    if kind in ("qk", "gm", "ga", "o", "if"):
                        if kind == "qk":
                            act.wait_ge(conv_out, j + 1)
                            if j:
                                act.wait_ge(qk_done, j)
                            nc.scalar.activation(t3[:], qk[:, j], ACT.Tanh, scale=0.5).then_inc(silu_th, 1)
                            return
                        act.wait_ge(evacuated[pos % 2], bank_uses(pos))
                        if kind == "gm":
                            nc.scalar.activation(th_gate[:, j], za[:, pos % 2], ACT.Tanh, scale=0.5).then_inc(gate_done, 1)
                        elif kind == "ga":
                            nc.scalar.activation(th_gate[:, KT + j], za[:, pos % 2], ACT.Tanh, scale=0.5).then_inc(gate_done, 1)
                        elif kind == "o":
                            if j >= 2:
                                act.wait_ge(head_gated, j - 1)
                            nc.scalar.activation(th_o[:, j % 2], za[:, pos % 2], ACT.Tanh, scale=0.5).then_inc(gate_done, 1)
                        else:
                            act.wait_ge(par_scaled, 1)
                            nc.scalar.activation(rows[:, 1], rows[:, 0], ACT.Tanh, scale=1.0 / CAP,
                                                 bias=small[0:2 * F_ROW, 15, 0:1]).then_inc(gate_th, 1)
                            act.wait_ge(gate_th, 1)
                            link(nc.scalar.activation(rows[0:M_HEADS, 0], rows[F_ROW:F_ROW + M_HEADS, 1], ACT.Exp, scale=-CAP))
                            nc.scalar.activation(rows[0:M_HEADS, 0], rows[0:M_HEADS, 0], ACT.Ln,
                                                 bias=ones[0:M_HEADS, 0:1]).then_inc(gate_sp, 1)

                def att_exponentials(c):
                    nk = CHUNK if c == 0 else 2 * CHUNK
                    act.wait_ge(logits_read, c + 1)
                    if c:
                        act.wait_ge(probs, c)
                    nc.scalar.activation(t1[:, 0:4 * nk], t0[:, 0:4 * nk], ACT.Exp).then_inc(att_exp, 1)
                    act.wait_ge(sink_gap, c + 1)
                    nc.scalar.activation(small[:, 3], small[:, 2], ACT.Exp).then_inc(att_exp, 1)

                def att_copy(c):
                    nk = CHUNK if c == 0 else 2 * CHUNK
                    act.wait_ge(probs_t, c + 1)
                    if c:
                        act.wait_ge(att_o, c)
                    else:
                        act.wait_ge(qk_done, 4)
                    nc.scalar.copy(t3[0:nk], b_pt[0:nk]).then_inc(probs_c, 1)

                def att_round(c):
                    act.wait_ge(att_o, c + 1)
                    nc.scalar.copy(hid[:, 0:4, 0, c * CHUNK:(c + 1) * CHUNK],
                                   b_av[:, 0:256].rearrange("p (a t) -> p a t", a=4)).then_inc(att_hi, 1)

                def mem_decay(h, S):
                    n = SEQ - S * P
                    act.wait_ge(decay_in, 4 * h + S + 1)
                    act.wait_ge(cols_done, 1)
                    if 4 * h + S:
                        act.wait_ge(weights, 4 * h + S)
                    nc.scalar.activation(t2[:, 0:n], b_lg[:, 0:n], ACT.Exp,
                                         bias=bcols[:, 4 * S + h:4 * S + h + 1]).then_inc(decay, 1)

                for w, (kind, j, pos) in enumerate(W_UNITS):
                    if w:
                        evacuation(w - 1)
                    if w == 7:
                        for i in range(2):
                            act.wait_ge(vwin_t, i + 1)
                            if i == 0:
                                nc.scalar.copy(vwin[0:CHUNK, 0], b_nm[0:CHUNK, 0:P]).then_inc(act_step, 1)
                                nc.scalar.copy(vwin[:, 1:4], b_nm[:, P:].rearrange("p (a d) -> p a d", a=3)).then_inc(vwin_done, 1)
                                steps[0] += 1
                            else:
                                nc.scalar.copy(vwin[:, 4:8], b_tr[:].rearrange("p (a d) -> p a d", a=4)).then_inc(vwin_done, 1)
                    if 12 <= w < 12 + M_HEADS:
                        h = w - 12
                        act.wait_ge(v_t, h + 1)
                        nc.scalar.copy(vn[:, h, :, 0:M_V], b_tr[:].rearrange("p (s d) -> p s d", s=TB)).then_inc(v_done, 1)
                    c = w - ATT0 - 1
                    if 0 <= c < NC:
                        att_exponentials(c)
                    if 0 <= c - 1 < NC:
                        att_copy(c - 1)
                    if 0 <= c - 2 < NC:
                        att_round(c - 2)
                    h, odd = divmod(w - MEM0, 2)
                    hf = h - 1
                    if 0 <= hf < M_HEADS and odd == 0:
                        for i in range(2):
                            act.wait_ge(summed, 4 * (hf + 1))
                            if hf:
                                act.wait_ge(head_t, hf)
                            nc.scalar.copy(hn[:, 2 * i:2 * i + 2], mem_banks[i][:, 0:2 * (M_V + 1)].rearrange(
                                "p (a d) -> p a d", a=2)).then_inc(sums_out, 1)
                    if 0 <= h < M_HEADS:
                        mem_decay(h, 2 * odd)
                    split_half(l, pos + 2, 0)
                    if 0 <= h < M_HEADS:
                        mem_decay(h, 2 * odd + 1)
                    split_half(l, pos + 2, 1)
                    if pos + 1 == NONE_POS:
                        for i in range(2):
                            split_half(l, pos + 3, i)
                    hg = h - 2
                    if 0 <= hg < M_HEADS and odd == 0:
                        act.wait_ge(head_gated, hg + 1)
                        nc.scalar.activation(hid[:, 4 + hg, 0], t0[:], ACT.Copy,
                                             scale=small[:, 14, hg:hg + 1]).then_inc(head_hi, 1)
                evacuation(len(W_UNITS) - 1)

                for m in range(KT):
                    for i in range(2):
                        split_half(l, BRANCH_POS + m + 2, i)
                    act.wait_ge(merged, m + 1)
                    nc.scalar.activation(xg_mix[:, m, 0], za[:, m % 2], ACT.Copy, scale=0.5).then_inc(merged_hi, 1)

                def new_x(m, n, dst, gcol):
                    if n < KT:
                        act.wait_ge(evacuated[(OUT_POS + m) % 2], bank_uses(OUT_POS + m))
                    else:
                        act.wait_ge(x_new, m + 1)
                    nc.scalar.activation(dst[:, m, 0], x[:, m], ACT.Copy, scale=par[:, gcol + m:gcol + m + 1]).then_inc(xg_hi, 1)
                    if n:
                        act.wait_ge(sq_sum, n)
                    nc.scalar.activation(sq_t[:], x[:, m], ACT.Square).then_inc(sq_done, 1)

                for m in range(KT):
                    for i in range(2):
                        split_half(l, OUT_POS + m + 2, i)
                    new_x(m, m, xg_mlp, PC_MLP_G)

                def mlp_quarter(q, last):
                    lay = (l, q)
                    for i in range(KT):
                        pos = MLP_POS + i
                        for half in range(2):
                            split_half(lay, pos + 2, half)
                        act.wait_ge(half_used, l * HALVES + q * (4 * KT) + (2 * (pos + 1) + 4))
                        nc.scalar.activation(pmat[:, i % 2], acc[pos % 2][:], ACT.Relu).then_inc(evacuated[pos % 2], 1)
                        act.wait_ge(relu_sq, q * KT + (i + 1))
                        nc.scalar.copy(hid[:, i, 0], za[:, i % 2]).then_inc(hid_hi, 1)
                    for m in range(KT):
                        pos = MLP_POS + KT + m
                        if not (last and m >= KT - 2):
                            for half in range(2):
                                split_half(lay, pos + 2, half)
                        if last:
                            new_x(m, KT + m, xg_mix, PC_NEXT_G)

                mlp_quarter(0, False)
                with act.Fori(1, QUARTERS - 1) as q:
                    mlp_quarter(q, False)
                mlp_quarter(QUARTERS - 1, True)
                act.drain().then_inc(at_rest, 1)

        @block.vector
        def _(dve):
            steps = [0]

            def link(ins):
                steps[0] += 1
                ins.then_inc(dve_step, 1)
                dve.wait_ge(dve_step, steps[0])

            def ts(o, a, s1, s2, op0, op1=None):
                return nc.vector.tensor_scalar(o, a, s1, s2, op0, op1) if op1 else nc.vector.tensor_scalar(o, a, s1, s2, op0)

            def stt(o, a, s, b, op0, op1):
                return nc.vector.scalar_tensor_tensor(out=o, in0=a, scalar=s, in1=b, op0=op0, op1=op1)

            def rsqrt(y, v):
                w, t = small[:, 11], small[:, 12]
                link(ts(smalli[:], v.bitcast(I32), 1, None, ALU.logical_shift_right))
                link(ts(y.bitcast(I32), smalli[:], -1.0, float(0x5F3759DF), ALU.mult, ALU.add))
                link(ts(w, v, -0.5, None, ALU.mult))
                for _ in range(3):
                    link(nc.vector.tensor_tensor(t, y, y, ALU.mult))
                    link(nc.vector.tensor_tensor(t, t, w, ALU.mult))
                    link(stt(y, t, 1.5, y, ALU.add, ALU.mult))

            def stat_diagonals(n, squared):
                dve.wait_ge(stat_sum, n)
                link(ts(small[:, 8], b_ms[:, 0:TB], 1.0 / D_MODEL, EPS, ALU.mult, ALU.add))
                rsqrt(small[:, 9], small[:, 8])
                if squared:
                    link(nc.vector.tensor_tensor(small[:, 9], small[:, 9], small[:, 9], ALU.mult))
                for c in range(TB):
                    ins = ts(ssum[:, c * P:(c + 1) * P], ident, small[:, 9, c:c + 1], None, ALU.mult)
                    ins.then_inc(stat_diag, 1)

            def stat_spread(n):
                dve.wait_ge(stat_bcast, n)
                nc.vector.tensor_copy(invb[:], b_ms[:]).then_inc(stat_done, 1)
                dve.wait_ge(stat_done, n)

            link(nc.vector.memset(ones[:], 1.0))
            link(nc.vector.memset(frows[:].bitcast(F32), 0.0))
            link(nc.vector.memset(vn[:], 1.0))
            dve.wait_ge(loaded, 96)
            link(nc.vector.tensor_copy(ident_r[:], ident))
            link(nc.vector.tensor_copy(mask_r[:], pmat[:, 0, 0:P]))
            link(nc.vector.tensor_copy(sel_r[:], pmat[0:2 * F_ROW, 1].rearrange("p (h m) -> p h m", h=M_HEADS)))
            link(nc.vector.tensor_copy(t3[:], pos_i))
            link(ts(t1[:], t3[:], cst[:, C_FREQ:C_FREQ + 1], None, ALU.mult))
            magic = 12582912.0
            link(ts(t2[:], t1[:], 0.15915494309189535, magic, ALU.mult, ALU.add))
            link(ts(t2[:], t2[:], -magic, None, ALU.add))
            for part in (6.28125, 0.0019340515136718750, 1.2556734959e-06):
                link(stt(t1[:], t2[:], -part, t1[:], ALU.mult, ALU.add))
            link(ts(t1[:], t1[:], 3.1415925, -3.1415925, ALU.min, ALU.max))
            link(stt(t2[:], t1[:], -1.0, t1[:], ALU.mult, ALU.max))
            dve.drain().then_inc(setup, 1)
            for m in range(KT):
                dve.wait_ge(setup, 4 + m)
                stt(xg_mix[:, m, 1], x[:, m], g0[:, m:m + 1], xg_mix[:, m, 0].bitcast(F32), ALU.mult, ALU.subtract).then_inc(dve_step, 1)
                steps[0] += 1
                dve.wait_ge(sq_done, m + 1)
                if m == 0:
                    nc.vector.tensor_copy(ssum[:], sq_t[:]).then_inc(sq_sum, 1)
                else:
                    nc.vector.tensor_tensor(ssum[:], ssum[:], sq_t[:], ALU.add).then_inc(sq_sum, 1)
                dve.wait_ge(sq_sum, m + 1)

            def next_layer(n):
                dve.drain()
                dve.wait_ge(at_rest, n)
                dve.nop(nofuse=True)
                for s in layer_sems:
                    dve.sem_clear(s)
                dve.nop(nofuse=True).then_inc(layer_go, 1)

            next_layer(1)
            with dve.Fori(0, DEPTH) as l:
                steps[0] = 0
                dve.wait_ge(layer_go, l + 1)
                dve.nop(nofuse=True)
                stat_diagonals(1, False)
                link(nc.vector.memset(conv_in[:, 0:TAPS - 1], 0.0))
                dve.wait_ge(par_in, l * 16 + 16)
                link(ts(small[:, 14], par[:, PC_HEAD_G:PC_HEAD_G + 4], 0.5, None, ALU.mult))
                ts(small[0:2 * F_ROW, 15, 0:1], par[0:2 * F_ROW, PC_GATE_B:PC_GATE_B + 1], 1.0 / CAP, None,
                   ALU.mult).then_inc(par_scaled, 1)

                def evacuation(w):
                    kind, j, pos = W_UNITS[w]
                    src, done = acc[pos % 2], evacuated[pos % 2]
                    if kind == "qk" and j:
                        dve.wait_ge(conv_out, j)
                    if kind == "qa":
                        dst, sc = qa[:, j], invb[:]
                    elif kind == "qk":
                        dst, sc = conv_in[:, TAPS - 1:], invb[:]
                    elif kind == "if":
                        dst, sc, src = rows[:, 0], invb[0:2 * F_ROW], acc[pos % 2][0:2 * F_ROW]
                    else:
                        dst, sc = za[:, pos % 2], invb[:]
                        if kind in ("gm", "ga", "o"):
                            earlier = [k for k, _, _ in W_UNITS[:w]]
                            n = sum(k in ("gm", "ga", "o") for k in earlier) - 1
                            if n >= 1:
                                dve.wait_ge(gate_done, n)
                            else:
                                dve.wait_ge(v_t, M_HEADS)
                        elif kind == "vm":
                            if j == 0:
                                dve.wait_ge(vwin_t, 2)
                                dve.wait_ge(roped, 5)
                            elif j >= 2:
                                dve.wait_ge(v_t, j - 1)
                    dve.wait_ge(half_used, unit_done(l, pos))
                    nc.vector.tensor_tensor(dst, src[:] if kind != "if" else src, sc, ALU.mult).then_inc(done, 1)
                    if kind == "qk":
                        dve.wait_ge(done, bank_uses(pos))
                        link(ts(qk[:, j], conv_in[:, 0:SEQ], par[:, PC_CONV + 4 * j:PC_CONV + 4 * j + 1], None, ALU.mult))
                        for t in range(1, TAPS):
                            col = PC_CONV + 4 * j + t
                            ins = stt(qk[:, j], conv_in[:, t:t + SEQ], par[:, col:col + 1], qk[:, j], ALU.mult, ALU.add)
                            if t < TAPS - 1:
                                link(ins)
                            else:
                                ins.then_inc(conv_out, 1)

                def silu(j):
                    dve.wait_ge(silu_th, j + 1)
                    stt(qk[:, j], t3[:], 1.0, qk[:, j], ALU.add, ALU.mult).then_inc(qk_done, 1)

                def rope(j):
                    src = qa[:, j] if j < 4 else za[:, 0]
                    dve.wait_ge(partner_ready, j + 1)
                    nc.vector.tensor_tensor(t1[:], b_ms[:], sin[:], ALU.mult).then_inc(partner_read, 1)
                    link(nc.vector.tensor_tensor(src, src, cos[:], ALU.mult))
                    dve.wait_ge(partner_read, j + 1)
                    if j < 4:
                        nc.vector.tensor_tensor(src, src, t1[:], ALU.add).then_inc(roped, 1)
                        dve.wait_ge(roped, j + 1)
                        return
                    for g in range(A_KV):
                        s = slice(64 * g, 64 * g + 64)
                        for e in range(2):
                            ins = nc.vector.tensor_tensor(kd[64 * e:64 * e + 64, g], za[s, 0], t1[s], ALU.add)
                            if g and e:
                                ins.then_inc(roped, 1)
                            else:
                                link(ins)
                    dve.wait_ge(roped, 5)

                def gate_rows():
                    dve.wait_ge(gate_sp, 1)
                    for S in range(TB):
                        link(nc.vector.tensor_tensor_scan(frow[:, SEG[S]:SEG[S + 1]], ones[0:M_HEADS, S * P:],
                                                          rows[0:M_HEADS, 0, S * P:], 0.0, ALU.mult, ALU.subtract))
                    for S in range(TB):
                        blk = slice(S * P, (S + 1) * P)
                        link(stt(rows[0:M_HEADS, 0, blk], rows[0:M_HEADS, 1, blk], CAP, frow[:, SEG[S]:SEG[S] + P],
                                 ALU.mult, ALU.subtract))
                    link(nc.vector.tensor_copy(frows[0:M_HEADS], frow[:]))
                    nc.vector.tensor_tensor(frows[F_ROW:F_ROW + M_HEADS], frow[:], frows[0:M_HEADS].bitcast(F32),
                                            ALU.subtract).then_inc(rows_done, 1)
                    dve.wait_ge(rows_done, 1)

                def gate_cols():
                    dve.wait_ge(cols_t, 1)
                    nc.vector.tensor_copy(bcols[:], b_tr[:, 0:TB * M_HEADS]).then_inc(cols_done, 1)
                    dve.wait_ge(cols_done, 1)

                def att_softmax(c):
                    nk = CHUNK if c == 0 else 2 * CHUNK
                    lg = b_lg[:, 0:4 * nk].rearrange("p (a k) -> p a k", a=4)
                    tv = t0[:, 0:4 * nk].rearrange("p (a k) -> p a k", a=4)
                    ev = t1[:, 0:4 * nk].rearrange("p (a k) -> p a k", a=4)
                    sink = par[:, PC_SINK:PC_SINK + 4]
                    dve.wait_ge(logits, c + 1)
                    link(nc.vector.tensor_reduce(small[:, 0], lg, AX.X, ALU.max))
                    link(stt(small[:, 1], small[:, 0], 0.125, sink, ALU.mult, ALU.max))
                    stt(tv, lg, 0.125, small[:, 1].unsqueeze(2).broadcast_to([P, 4, nk]),
                        ALU.mult, ALU.subtract).then_inc(logits_read, 1)
                    nc.vector.tensor_tensor(small[:, 2], sink, small[:, 1], ALU.subtract).then_inc(sink_gap, 1)
                    dve.wait_ge(att_exp, 2 * c + 2)
                    link(nc.vector.tensor_reduce(small[:, 4], ev, AX.X, ALU.add))
                    link(nc.vector.tensor_tensor(small[:, 4], small[:, 4], small[:, 3], ALU.add))
                    link(nc.vector.reciprocal(small[:, 5], small[:, 4]))
                    if c:
                        dve.wait_ge(probs_t, c)
                    nc.vector.tensor_tensor(pmat[:, 0, 0:4 * nk].rearrange("p (a k) -> p a k", a=4), ev,
                                            small[:, 5].unsqueeze(2).broadcast_to([P, 4, nk]), ALU.mult).then_inc(probs, 1)
                    dve.wait_ge(probs, c + 1)

                def att_rest(c):
                    dve.wait_ge(att_hi, c + 1)
                    dst = hid[:, 0:4, :, c * CHUNK:(c + 1) * CHUNK]
                    nc.vector.tensor_tensor(dst[:, :, 1], b_av[:, 0:256].rearrange("p (a t) -> p a t", a=4),
                                            dst[:, :, 0].bitcast(F32), ALU.subtract).then_inc(att_lo, 1)

                def mem_weights(h, S):
                    n = SEQ - S * P
                    i = 4 * h + S
                    dve.wait_ge(scores_in, i + 1)
                    dve.wait_ge(decay, i + 1)
                    if i >= 2:
                        dve.wait_ge(summed, i - 1)
                    if i < 2:
                        dve.wait_ge(probs_t, NC)
                    stt(pmat[:, i % 2, 0:n], b_pt[:, 0:n], 0.25 * M_QK ** -0.5, t2[:, 0:n], ALU.mult, ALU.mult).then_inc(weights, 1)

                def head_normalise(h):
                    dve.wait_ge(sums_out, 2 * h + 2)
                    den, rd, ms = small[:, 4], small[:, 5], small[:, 6]
                    num = hn[:, :, 0:M_V]
                    link(stt(den, hn[:, :, M_V], -1.0, hn[:, :, M_V], ALU.mult, ALU.max))
                    link(ts(den, den, 1.0, None, ALU.max))
                    link(nc.vector.reciprocal(rd, den))
                    tv = t1[:].rearrange("p (a d) -> p a d", a=TB)
                    link(nc.vector.tensor_tensor(tv, num, num, ALU.mult))
                    link(nc.vector.tensor_reduce(ms, tv, AX.X, ALU.add))
                    link(nc.vector.tensor_tensor(ms, ms, rd, ALU.mult))
                    link(nc.vector.tensor_tensor(ms, ms, rd, ALU.mult))
                    link(ts(ms, ms, 1.0 / M_V, EPS, ALU.mult, ALU.add))
                    rsqrt(small[:, 7], ms)
                    link(nc.vector.tensor_tensor(rd, rd, small[:, 7], ALU.mult))
                    nc.vector.tensor_tensor(num, num, rd.unsqueeze(2).broadcast_to([P, TB, M_V]), ALU.mult).then_inc(head_norm, 1)
                    dve.wait_ge(head_norm, h + 1)

                def head_gate(h):
                    dve.wait_ge(head_t, h + 1)
                    n_o = [i for i, (k, jj, _) in enumerate([u for u in W_UNITS if u[0] in ("gm", "ga", "o")]) if k == "o" and jj == h][0]
                    dve.wait_ge(gate_done, n_o + 1)
                    stt(t0[:], th_o[:, h % 2], 1.0, b_tr[:], ALU.add, ALU.mult).then_inc(head_gated, 1)
                    dve.wait_ge(head_hi, h + 1)
                    stt(hid[:, 4 + h, 1], t0[:], small[:, 14, h:h + 1], hid[:, 4 + h, 0].bitcast(F32),
                        ALU.mult, ALU.subtract).then_inc(head_lo, 1)
                    dve.wait_ge(head_lo, h + 1)

                for w, (kind, j, pos) in enumerate(W_UNITS):
                    if w == 1:
                        stat_spread(1)
                    if w:
                        evacuation(w - 1)
                    if 2 <= w < 7:
                        rope(w - 2)
                    if w >= 8 and W_UNITS[w - 2][0] == "qk":
                        silu(W_UNITS[w - 2][1])
                    c = w - ATT0 - 1
                    if 0 <= c < NC:
                        att_softmax(c)
                    if 0 <= c - 2 < NC:
                        att_rest(c - 2)
                    if w == 16:
                        gate_rows()
                    if w == 18:
                        gate_cols()
                    h, odd = divmod(w - MEM0, 2)
                    if 0 <= h < M_HEADS:
                        mem_weights(h, 2 * odd)
                        mem_weights(h, 2 * odd + 1)
                    if odd == 0 and 0 <= h - 2 < M_HEADS:
                        head_gate(h - 2)
                    if odd == 0 and 0 <= h - 1 < M_HEADS:
                        head_normalise(h - 1)
                evacuation(len(W_UNITS) - 1)
                n_gates = sum(u[0] in ("gm", "ga", "o") for u in W_UNITS)

                for m in range(KT):
                    pos = BRANCH_POS + m
                    z = za[:, m % 2]
                    dve.wait_ge(gate_done, n_gates)
                    dve.wait_ge(half_used, unit_done(l, pos))
                    stt(z, th_gate[:, KT + m], 1.0, acc[pos % 2][:], ALU.add, ALU.mult).then_inc(evacuated[pos % 2], 1)
                    stt(t0[:], th_gate[:, m], 1.0, branch_banks[m % 2][:], ALU.add, ALU.mult).then_inc(second_read, 1)
                    dve.wait_ge(second_read, m + 1)
                    nc.vector.tensor_tensor(z, z, t0[:], ALU.add).then_inc(merged, 1)
                    dve.wait_ge(merged_hi, m + 1)
                    stt(xg_mix[:, m, 1], z, 0.5, xg_mix[:, m, 0].bitcast(F32), ALU.mult, ALU.subtract).then_inc(merged_lo, 1)

                def new_x(m, n, dst, gcol):
                    dve.wait_ge(xg_hi, n + 1)
                    stt(dst[:, m, 1], x[:, m], par[:, gcol + m:gcol + m + 1], dst[:, m, 0].bitcast(F32),
                        ALU.mult, ALU.subtract).then_inc(xg_lo, 1)
                    dve.wait_ge(sq_done, n + 1)
                    if m == 0:
                        nc.vector.tensor_copy(ssum[:], sq_t[:]).then_inc(sq_sum, 1)
                    else:
                        nc.vector.tensor_tensor(ssum[:], ssum[:], sq_t[:], ALU.add).then_inc(sq_sum, 1)
                    dve.wait_ge(sq_sum, n + 1)

                for m in range(KT):
                    pos = OUT_POS + m
                    dve.wait_ge(half_used, unit_done(l, pos))
                    nc.vector.tensor_tensor(x[:, m], x[:, m], acc[pos % 2][:], ALU.add).then_inc(evacuated[pos % 2], 1)
                    dve.wait_ge(evacuated[pos % 2], bank_uses(pos))
                    new_x(m, m, xg_mlp, PC_MLP_G)

                def mlp_quarter(q, first, last):
                    for i in range(KT):
                        pos = MLP_POS + i
                        if first and i == 2:
                            stat_diagonals(2, True)
                        if first and i == 4:
                            stat_spread(2)
                        dve.wait_ge(evacuated[pos % 2], q * KT + bank_uses(pos))
                        if i >= 2:
                            dve.wait_ge(hid_lo, q * KT + (i - 1))
                        nc.vector.tensor_tensor(za[:, i % 2], pmat[:, i % 2], pmat[:, i % 2], ALU.mult).then_inc(relu_sq, 1)
                        dve.wait_ge(hid_hi, q * KT + (i + 1))
                        nc.vector.tensor_tensor(hid[:, i, 1], za[:, i % 2], hid[:, i, 0].bitcast(F32), ALU.subtract).then_inc(hid_lo, 1)
                        if i == KT - 1:
                            dve.wait_ge(hid_lo, q * KT + KT)
                    for m in range(KT):
                        pos = MLP_POS + KT + m
                        dve.wait_ge(half_used, l * HALVES + q * (4 * KT) + (2 * (pos + 1) + 4))
                        nc.vector.tensor_tensor(t0[:], acc[pos % 2][:], invb[:], ALU.mult).then_inc(evacuated[pos % 2], 1)
                        dve.wait_ge(evacuated[pos % 2], q * KT + bank_uses(pos))
                        nc.vector.tensor_tensor(x[:, m], x[:, m], t0[:], ALU.add).then_inc(x_new if last else down_scaled, 1)
                        if last:
                            dve.wait_ge(x_new, m + 1)
                            new_x(m, KT + m, xg_mix, PC_NEXT_G)
                        else:
                            dve.wait_ge(down_scaled, q * KT + (m + 1))

                mlp_quarter(0, True, False)
                with dve.Fori(1, QUARTERS - 1) as q:
                    mlp_quarter(q, False, False)
                mlp_quarter(QUARTERS - 1, False, True)
                next_layer(2 * l + 3)

            steps[0] = 0
            stat_diagonals(1, False)
            stat_spread(1)
            for m in range(KT):
                stt(x[:, m], x[:, m], par[:, PC_NEXT_G + m:PC_NEXT_G + m + 1], invb[:], ALU.mult, ALU.mult).then_inc(final_out, 1)

        @block.tensor
        def _(pe):
            pe.sem_inc(half_used, 4)

            def stat_sums():
                for c in range(TB):
                    last = nc.tensor.matmul(b_ms[:, c:c + 1], ssum[:, c * P:(c + 1) * P], ones[:, 0:1], start=True, stop=True)
                last.then_inc(stat_sum, 1)

            def stat_rows(n):
                pe.wait_ge(stat_diag, TB * n)
                nc.tensor.matmul(b_ms[:], ones[:, 0:P], ssum[:], start=True, stop=True).then_inc(stat_bcast, 1)

            with pe.Fori(0, DEPTH) as l:
                pe.wait_ge(layer_go, l + 1)
                stat_sums()

                def unit_start(pos):
                    if bank_uses(pos) > 1:
                        pe.wait_ge(evacuated[pos % 2], bank_uses(pos) - 1)

                def unit_half(pos, i, rhs, ready=None, bank=None, whole=True):
                    pe.wait_ge(lo_done, l * HALVES + (2 * pos + i + 1))
                    s = (2 * pos + i) % 4
                    b = acc[pos % 2] if bank is None else bank
                    for k in range(4):
                        kk = 4 * i + k
                        if ready is not None:
                            pe.wait_ge(ready, kk + 1)
                        for q, (wt, a) in enumerate(((whi, 0), (whi, 1), (wlo, 0))):
                            last = nc.tensor.matmul(b[:], wt[:, s, k], rhs[:, kk, a],
                                                    start=(k == 0 and q == 0 and (i == 0 or not whole)),
                                                    stop=(k == 3 and q == 2 and (i == 1 or not whole)))
                    last.then_inc(half_used, 1)

                def partner(j):
                    kind, _, pos = W_UNITS[j]
                    pe.wait_ge(evacuated[pos % 2], bank_uses(pos))
                    if j:
                        pe.wait_ge(partner_read, j)
                    src = qa[:, j] if j < 4 else za[:, 0]
                    nc.tensor.matmul(b_ms[:], cst[:, C_ROPE:C_ROPE + P], src, start=True, stop=True).then_inc(partner_ready, 1)

                def value_windows():
                    pos = W_UNITS[5][2]
                    pe.wait_ge(evacuated[pos % 2], bank_uses(pos))
                    v = za[:, 1]
                    nc.tensor.transpose(b_nm[0:CHUNK, 0:P], v[:, 0:CHUNK], ident)
                    for c in range(1, NC):
                        bank = b_nm if c < 4 else b_tr
                        last = nc.tensor.transpose(bank[:, (c % 4) * P:(c % 4 + 1) * P], v[:, (c - 1) * CHUNK:(c + 1) * CHUNK], ident)
                        if c % 4 == 3:
                            last.then_inc(vwin_t, 1)

                def turn_values(h):
                    pos = W_UNITS[10 + h][2]
                    pe.wait_ge(evacuated[pos % 2], bank_uses(pos))
                    if h == 0:
                        pe.wait_ge(vwin_done, 2)
                    else:
                        pe.wait_ge(v_done, h)
                    for S in range(TB):
                        last = nc.tensor.transpose(b_tr[:, S * P:(S + 1) * P], za[:, pos % 2, S * P:(S + 1) * P], ident)
                    last.then_inc(v_t, 1)

                def turn_columns():
                    pe.wait_ge(rows_done, 1)
                    pe.wait_ge(v_done, M_HEADS)
                    for S in range(TB):
                        last = nc.tensor.transpose(b_tr[:, S * M_HEADS:(S + 1) * M_HEADS], rows[0:M_HEADS, 0, S * P:(S + 1) * P],
                                                   cst[0:M_HEADS, C_ID:C_ID + M_HEADS])
                    last.then_inc(cols_t, 1)

                def att_logits(c):
                    nk = CHUNK if c == 0 else 2 * CHUNK
                    k0 = max(c - 1, 0) * CHUNK
                    if c == 0:
                        pe.wait_ge(roped, 5)
                    else:
                        pe.wait_ge(logits_read, c)
                    for a in range(PAIRS_H):
                        for e in range(2):
                            s = slice(64 * e, 64 * e + 64)
                            last = nc.tensor.matmul(b_lg[s, a * nk:(a + 1) * nk], qa[s, a, c * CHUNK:(c + 1) * CHUNK],
                                                    kd[s, a // 2, k0:k0 + nk], start=True, stop=True)
                    last.then_inc(logits, 1)

                def att_turn(c):
                    nk = CHUNK if c == 0 else 2 * CHUNK
                    pe.wait_ge(probs, c + 1)
                    if c:
                        pe.wait_ge(probs_c, c)
                    for a in range(PAIRS_H):
                        last = nc.tensor.transpose(b_pt[0:nk, a * P:(a + 1) * P], pmat[:, 0, a * nk:(a + 1) * nk], ident)
                    last.then_inc(probs_t, 1)

                def att_values(c):
                    nk = CHUNK if c == 0 else 2 * CHUNK
                    pe.wait_ge(probs_c, c + 1)
                    if c == 0:
                        pe.wait_ge(vwin_done, 2)
                    else:
                        pe.wait_ge(att_lo, c)
                    pv = t3[0:nk].rearrange("p (a e t) -> p a e t", a=PAIRS_H, e=2)
                    for g in range(A_KV):
                        for e in range(2):
                            last = nc.tensor.matmul(b_av[64 * e:64 * e + 64, g * 2 * CHUNK:(g + 1) * 2 * CHUNK],
                                                    vwin[0:nk, c, g * A_DIM:(g + 1) * A_DIM], pv[:, 2 * g:2 * g + 2, e],
                                                    start=True, stop=True)
                    last.then_inc(att_o, 1)

                def mem_inputs(h, S):
                    i = 4 * h + S
                    n = SEQ - S * P
                    if i == 0:
                        pe.wait_ge(rows_done, 1)
                        pe.wait_ge(logits_read, NC)
                        pe.wait_ge(probs_c, NC)
                        pe.wait_ge(qk_done, 4)
                    else:
                        pe.wait_ge(decay, i)
                    nc.tensor.matmul(b_lg[:, 0:n], sel_r[:, h], frows[:, SEG[S]:SEG[S + 1]], start=True, stop=True,
                                 skip_group_check=True)
                    nc.tensor.matmul(b_lg[:, 0:P], ident_r[:], mask_r[:], start=False, stop=True,
                                     skip_group_check=True).then_inc(decay_in, 1)
                    if i:
                        pe.wait_ge(weights, i)
                    s = slice(head_part(h), head_part(h) + M_QK)
                    nc.tensor.matmul(b_pt[:, 0:n], qk[s, 2 + h // 2, S * P:(S + 1) * P], qk[s, h // 2, S * P:SEQ],
                                     start=True, stop=True).then_inc(scores_in, 1)

                def mem_sums(h, S):
                    i = 4 * h + S
                    pe.wait_ge(weights, i + 1)
                    if S == 0 and h:
                        pe.wait_ge(sums_out, 2 * h)
                    if i == 0:
                        pe.wait_ge(vwin_done, 2)
                    for T in range(S, TB):
                        bank = mem_banks[T // 2]
                        last = nc.tensor.matmul(bank[:, (T % 2) * (M_V + 1):(T % 2 + 1) * (M_V + 1)],
                                                pmat[:, i % 2, (T - S) * P:(T - S + 1) * P], vn[:, h, S, :],
                                                start=(S == 0 and T % 2 == 0), stop=(S == T), skip_group_check=True)
                    last.then_inc(summed, 1)

                def turn_head(h):
                    pe.wait_ge(head_norm, h + 1)
                    if h:
                        pe.wait_ge(head_gated, h)
                    else:
                        pe.wait_ge(cols_done, 1)
                    for T in range(TB):
                        last = nc.tensor.transpose(b_tr[:, T * P:(T + 1) * P], hn[:, T, 0:M_V], ident)
                    last.then_inc(head_t, 1)

                for w, (kind, j, pos) in enumerate(W_UNITS):
                    h, odd = divmod(w - MEM0, 2)
                    mem = 0 <= h < M_HEADS
                    if mem:
                        mem_inputs(h, 2 * odd)
                    unit_start(pos)
                    unit_half(pos, 0, xg_mix)
                    if mem:
                        mem_sums(h, 2 * odd)
                        mem_inputs(h, 2 * odd + 1)
                    unit_half(pos, 1, xg_mix)
                    if mem:
                        mem_sums(h, 2 * odd + 1)
                    if pos + 1 == NONE_POS:
                        pe.wait_ge(lo_done, l * HALVES + 2 * (NONE_POS + 1))
                        pe.nop(nofuse=True)
                        pe.drain().then_inc(half_used, 2)
                    if w == 0:
                        stat_rows(1)
                    if 1 <= w < 6:
                        if w == 1:
                            pe.wait_ge(stat_done, 1)
                        partner(w - 1)
                    if w == 6:
                        value_windows()
                    if 11 <= w < 11 + M_HEADS:
                        turn_values(w - 11)
                    if w == 17:
                        turn_columns()
                    c = w - ATT0
                    if 0 <= c - 2 < NC:
                        att_values(c - 2)
                    if 0 <= c - 1 < NC:
                        att_turn(c - 1)
                    if 0 <= c < NC:
                        att_logits(c)
                    if 0 <= h - 1 < M_HEADS and odd == 1:
                        turn_head(h - 1)

                for m in range(KT):
                    pos = BRANCH_POS + m
                    unit_start(pos)
                    if m == 0:
                        pe.wait_ge(att_lo, NC)
                    unit_half(pos, 0, hid, whole=False)
                    if m == 0:
                        pe.wait_ge(head_lo, M_HEADS)
                    if m >= 2:
                        pe.wait_ge(second_read, m - 1)
                    unit_half(pos, 1, hid, bank=branch_banks[m % 2], whole=False)

                for m in range(KT):
                    pos = OUT_POS + m
                    unit_start(pos)
                    for i in range(2):
                        unit_half(pos, i, xg_mix, ready=merged_lo if m == 0 else None)

                def mlp_unit(q, pos, rhs, ready, base):
                    pe.wait_ge(evacuated[pos % 2], q * KT + (bank_uses(pos) - 1))
                    for i in range(2):
                        pe.wait_ge(lo_done, l * HALVES + q * (4 * KT) + (2 * pos + i + 1))
                        s = (2 * pos + i) % 4
                        for k in range(4):
                            kk = 4 * i + k
                            if ready is not None:
                                pe.wait_ge(ready, base + (kk + 1))
                            for t, (wt, a) in enumerate(((whi, 0), (whi, 1), (wlo, 0))):
                                last = nc.tensor.matmul(acc[pos % 2][:], wt[:, s, k], rhs[:, kk, a],
                                                        start=(kk == 0 and t == 0), stop=(kk == KT - 1 and t == 2))
                        last.then_inc(half_used, 1)

                def mlp_quarter(q, first):
                    for i in range(KT):
                        mlp_unit(q, MLP_POS + i, xg_mlp, xg_lo if first and i == 0 else None, 0)
                        if first and i == 1:
                            pe.wait_ge(sq_sum, KT)
                            stat_sums()
                        if first and i == 3:
                            stat_rows(2)
                    for m in range(KT):
                        mlp_unit(q, MLP_POS + KT + m, hid, hid_lo if m == 0 else None, q * KT)

                mlp_quarter(0, True)
                with pe.Fori(1, QUARTERS - 1) as q:
                    mlp_quarter(q, False)
                mlp_quarter(QUARTERS - 1, False)
                pe.drain().then_inc(at_rest, 1)

            pe.wait_ge(layer_go, DEPTH + 1)
            stat_sums()
            stat_rows(1)


_OUT = (D_MODEL, SEQ)


def kernel(**inputs):
    import numpy as np
    import concourse.bacc as bacc
    from concourse import mybir as mb
    from concourse.bass_utils import run_bass_kernel_spmd

    a = {n: np.asarray(v) for n, v in inputs.items()}

    cst = np.zeros((P, CCOLS), np.float32)
    cst[:, C_ID:C_ID + P] = np.eye(P)
    cst[:, C_MASK:C_MASK + P] = np.tril(np.full((P, P), MASKED), -1)
    half = ROT_DIM // 2
    for head in range(2):
        for i in range(half):
            lo, hi = head * A_DIM + i, head * A_DIM + half + i
            cst[hi, C_ROPE + lo] = -1.0
            cst[lo, C_ROPE + hi] = 1.0
            cst[[lo, hi], C_FREQ] = np.float32(ROPE_THETA) ** np.float32(-2 * i / ROT_DIM)
    for h in range(M_HEADS):
        cst[[h, F_ROW + h], C_SEL + h * P:C_SEL + (h + 1) * P] = 1.0
    cst[:, C_HALFPI] = np.pi / 2

    w_in = a["w_in"]
    widths = (("qk", 4 * P), ("vm", 4 * P), ("if", 2 * M_HEADS), ("o", 4 * P), ("qa", 4 * P), ("ka", P), ("va", P),
              ("gm", 8 * P), ("ga", 8 * P))
    first, at = {}, 0
    for kind, width in widths:
        first[kind] = at
        at += width
    stream = np.zeros((DEPTH, PAIRS, P, KT, 2, P), np.float32)

    def put(lay, pos, w):
        stream[lay, pos // 2, :, :, pos % 2, :] = w.reshape(KT, P, P).transpose(1, 0, 2)

    for lay in range(DEPTH):
        for kind, j, pos in W_UNITS:
            if kind == "if":
                gates = np.zeros((D_MODEL, P), np.float32)
                c = first["if"]
                gates[:, 0:M_HEADS] = w_in[lay][:, c:c + M_HEADS]
                gates[:, F_ROW:F_ROW + M_HEADS] = w_in[lay][:, c + M_HEADS:c + 2 * M_HEADS]
                put(lay, pos, gates)
            else:
                c = first[kind] + j * P
                put(lay, pos, w_in[lay][:, c:c + P])
        both = np.concatenate([a["w_branch_a"][lay], a["w_branch_m"][lay]], axis=0)
        for m in range(KT):
            cols = slice(m * P, (m + 1) * P)
            put(lay, BRANCH_POS + m, both[:, cols])
            put(lay, OUT_POS + m, a["w_out"][lay][:, cols])
        for q in range(QUARTERS):
            for m in range(KT):
                c = (q * KT + m) * P
                put(lay, MLP_POS + 2 * KT * q + m, a["w_up"][lay][:, c:c + P])
                put(lay, MLP_POS + 2 * KT * q + KT + m,
                    a["w_down"][lay][q * D_MODEL:(q + 1) * D_MODEL, m * P:(m + 1) * P])

    gains = np.concatenate([a["norm_mix_g"][1:], a["final_norm_g"][None]], axis=0)
    par = np.zeros((DEPTH, P, PCOLS), np.float32)
    for lay in range(DEPTH):
        par[lay, :, PC_CONV:PC_CONV + 16] = a["conv_qk_w"][lay].T.reshape(4, P, TAPS).transpose(1, 0, 2).reshape(P, 16)
        par[lay, :, PC_MLP_G:PC_MLP_G + KT] = a["norm_mlp_g"][lay].reshape(KT, P).T
        par[lay, :, PC_NEXT_G:PC_NEXT_G + KT] = gains[lay].reshape(KT, P).T
        par[lay, :, PC_HEAD_G:PC_HEAD_G + 4] = a["mlstm_norm_g"][lay].reshape(4, P).T
        par[lay, 0:M_HEADS, PC_GATE_B] = a["mlstm_gate_b"][lay][:M_HEADS]
        par[lay, F_ROW:F_ROW + M_HEADS, PC_GATE_B] = a["mlstm_gate_b"][lay][M_HEADS:]
        par[lay, :, PC_SINK:PC_SINK + 4] = np.repeat(a["attn_sinks"][lay].reshape(4, 2).T, CHUNK, axis=0)

    arrays = {
        "x_t": np.ascontiguousarray(a["x"][0].T),
        "positions": np.ascontiguousarray(a["positions"]),
        "consts": cst,
        "params": par,
        "g_first": np.ascontiguousarray(a["norm_mix_g"][0].reshape(KT, P).T),
        "w_stream": stream.reshape(DEPTH * PAIRS, P, KT, 2 * P),
    }
    nc = bacc.Bacc("TRN2", target_bir_lowering=False, num_devices=1)
    args = [nc.dram_tensor(n, v.shape, mb.dt.from_np(v.dtype), kind="ExternalInput").ap() for n, v in arrays.items()]
    out = nc.dram_tensor("y_t", _OUT, mb.dt.float32, kind="ExternalOutput").ap()
    program(nc, *args, out)
    r = run_bass_kernel_spmd(nc, [arrays], core_ids=[0])
    return np.ascontiguousarray(r.results[0]["y_t"].T)[None]
```

```python
from contextlib import ExitStack

import concourse.bass as bass
from concourse import mybir

F32 = mybir.dt.float32
F32R = mybir.dt.float32r
I32 = mybir.dt.int32
ALU = mybir.AluOpType
ACT = mybir.ActivationFunctionType
AX = mybir.AxisListType

P = 128
SEQ, D_MODEL, DEPTH = 512, 1024, 2
KT = D_MODEL // P
TB = SEQ // P
CHUNK = 64
NC = SEQ // CHUNK
M_HEADS, M_QK, M_V, TAPS = 4, 64, 128, 4
A_HEADS, A_KV, A_DIM = 8, 2, 64
PAIRS_H = A_HEADS // 2
F_TILES = 4 * D_MODEL // P
QUARTERS = F_TILES // KT
EPS = 1e-6
CAP = 15.0
MASKED = -1e30
ROT_DIM, ROPE_THETA = A_DIM // 4, 500000.0

W_ORDER = (["qa"] * 4 + ["ka", "va"] + ["qk"] * 4 + ["vm"] * 4 + ["if", "none"] + ["gm"] * 8
           + ["o"] * 2 + ["ga"] * 2 + ["o"] * 2 + ["ga"] * 6)
W_UNITS = [(kind, W_ORDER[:n].count(kind), n) for n, kind in enumerate(W_ORDER) if kind != "none"]
NONE_POS = W_ORDER.index("none")
BRANCH_POS = len(W_ORDER)
OUT_POS = BRANCH_POS + KT
MLP_POS = OUT_POS + KT
UNITS = MLP_POS + 2 * F_TILES
PAIRS = UNITS // 2
HALVES = 2 * UNITS
F_ROW = 32

PC_CONV, PC_MLP_G, PC_NEXT_G, PC_HEAD_G, PC_GATE_B, PC_SINK = 0, 16, 24, 32, 36, 37
PCOLS = 41
C_ID, C_SIGN, C_FREQ, C_HALFPI, C_GAIN = 0, P, P + 1, P + 2, P + 3
CKEPT = C_GAIN + KT
C_MASK, C_SEL = CKEPT, CKEPT + P
CCOLS = C_SEL + M_HEADS * P
PARTNER = [(i + ROT_DIM // 2) % ROT_DIM if i < ROT_DIM else i for i in range(32)]
ROPE_ORDER = [0, 1, 4, 2, 3]
ROPE_SLOT = {4: [0, 1], 5: [2], 6: [3], 7: [4]}

ATT0 = 10
MEM0 = 22
SEG = [0, 512, 896, 1152, 1280]


def bank_of(pos):
    return (0, 2, 3, 1)[pos] if pos < 4 else pos % 2


def bank_uses(pos):
    return sum(bank_of(p) == bank_of(pos) for p in range(pos + 1) if p != NONE_POS)


def program(nc, xt, pos_in, consts, params, wstream, out):
    with ExitStack() as ctx:
        layer_sems = []

        def sem(name):
            return ctx.enter_context(nc.semaphore(name))

        def lsem(name):
            s = sem(name)
            layer_sems.append(s)
            return s

        def sb(name, shape, dt=F32, where=ctx):
            return where.enter_context(nc.sbuf_tensor(name, shape, dt))

        x = sb("x", [P, KT, SEQ])
        xg_mix = sb("xg_mix", [P, KT, 2, SEQ], F32R)
        with ExitStack() as early:
            th_gate = sb("th_gate", [P, 2 * KT, SEQ], F32, early)
        xg_mlp = sb("xg_mlp", [P, KT, 2, SEQ], F32R)
        with ExitStack() as early:
            sb("skip_ha", [P, KT // 2, 2, SEQ], F32, early)
            qa = sb("qa", [P, PAIRS_H, SEQ], F32, early)
            with ExitStack() as first:
                kd = sb("kd", [P, A_KV, SEQ], F32, first)
                vwin = sb("vwin", [P, NC, P], F32, first)
            qk_hi = sb("qk_hi", [P, 4, SEQ], F32R, early)
        hid = sb("hid", [P, KT, 2, SEQ], F32R)
        raw = sb("raw", [P, 2, KT, 2 * P])
        whi = sb("whi", [P, 4, KT // 2, P], F32R)
        wlo = sb("wlo", [P, 4, KT // 2, P], F32R)
        cst = sb("cst", [P, CKEPT])
        par = sb("par", [P, PCOLS])
        ident_r = sb("ident_r", [P, P], F32R)
        mask_r = sb("mask_r", [P, P], F32R)
        sel_r = sb("sel_r", [2 * F_ROW, M_HEADS, P], F32R)
        ones = sb("ones", [P, SEQ])
        cos = sb("cos", [P, SEQ])
        sin = sb("sin", [P, SEQ])
        invb = sb("invb", [P, SEQ])
        ssum = sb("ssum", [P, SEQ])
        za = sb("za", [P, 2, SEQ])
        with ExitStack() as early:
            qk = sb("qk", [P, 4, SEQ], F32, early)
        qk_lo = sb("qk_lo", [P, 4, SEQ], F32R)
        vn = sb("vn", [P, M_HEADS, TB, M_V + 1])
        frows = sb("frows", [2 * F_ROW, SEG[-1]], F32R)
        with ExitStack() as early:
            rows = sb("rows", [2 * F_ROW, 2, SEQ], F32, early)
        hn = sb("hn", [P, TB, M_V + 1])
        sb("rows_rest", [P, 2 * SEQ - TB * (M_V + 1)])
        bcols = sb("bcols", [P, TB * M_HEADS])
        turns = sb("turns", [P, SEG[-1]])
        conv_in = turns[:, 0:TAPS - 1 + SEQ]
        frow = turns[0:M_HEADS]
        th_o = turns[:, 0:2 * SEQ].rearrange("p (a t) -> p a t", a=2)
        t0 = sb("t0", [P, SEQ])
        t1 = sb("t1", [P, SEQ])
        t2 = sb("t2", [P, SEQ])
        t3 = sb("t3", [P, SEQ])
        pmat = sb("pmat", [P, 2, SEQ])
        small = sb("small", [P, 16, TB])
        smalli = sb("smalli", [P, TB], I32)
        sq_t = t3
        first_sq = [ssum[:]] + [qk[:, j] for j in range(4)] + [za[:, j] for j in range(2)] + [sq_t[:]]
        pos_i = t0[:].bitcast(I32)
        ident = cst[:, C_ID:C_ID + P]

        def ps(name):
            return ctx.enter_context(nc.psum_tensor(name, [P, 512], F32))

        acc = [ps("acc0"), ps("acc1")]
        b_lg = ps("b_lg")
        b_pt = ps("b_pt")
        b_av = ps("b_av")
        b_ms = ps("b_ms")
        b_nm = ps("b_nm")
        b_tr = ps("b_tr")
        mem_banks = [b_ms, b_nm]
        branch_banks = [b_lg, b_pt]
        acc += branch_banks

        raw_in = [sem("raw_in0"), sem("raw_in1")]
        hi_done = sem("hi_done")
        lo_done = sem("lo_done")
        half_used = sem("half_used")
        par_in = sem("par_in")
        consts_in, pos_landed = sem("consts_in"), sem("pos_landed")
        rounding_in = sem("rounding_in")
        x_in = [sem(f"x_in{k}") for k in range(KT)]
        constants = sem("constants")
        setup = sem("setup")
        angles, tables = sem("angles"), sem("tables")
        first_hi = sem("first_hi")
        first_square, pool_squares = sem("first_square"), sem("pool_squares")
        final_squares, final_sum = sem("final_squares"), sem("final_sum")
        mix_lo = sem("mix_lo")
        stored = sem("stored")
        layer_go = sem("layer_go")
        at_rest = sem("at_rest")
        dve_step, act_step = lsem("dve_step"), lsem("act_step")
        evacuated = [lsem(f"evacuated{b}") for b in range(4)]
        stat_sum, stat_diag, stat_bcast, stat_done = lsem("stat_sum"), lsem("stat_diag"), lsem("stat_bcast"), lsem("stat_done")
        roped = lsem("roped")
        vwin_t, vwin_done = lsem("vwin_t"), lsem("vwin_done")
        conv_out, silu_th, qk_done = lsem("conv_out"), lsem("silu_th"), lsem("qk_done")
        qk_rounded, qk_split = lsem("qk_rounded"), lsem("qk_split")
        v_t, v_done = lsem("v_t"), lsem("v_done")
        gate_th, gate_sp = lsem("gate_th"), lsem("gate_sp")
        rows_done, cols_t, cols_done = lsem("rows_done"), lsem("cols_t"), lsem("cols_done")
        logits, logits_read, att_exp, probs, probs_t, probs_c, att_o, att_hi, att_lo = (
            lsem(n) for n in ("logits", "logits_read", "att_exp", "probs", "probs_t", "probs_c", "att_o", "att_hi", "att_lo"))
        sink_gap = lsem("sink_gap")
        decay_in, scores_in, decay, weights, summed = (
            lsem(n) for n in ("decay_in", "scores_in", "decay", "weights", "summed"))
        sums_out, head_norm, head_t, head_gated, head_hi, head_lo = (
            lsem(n) for n in ("sums_out", "head_norm", "head_t", "head_gated", "head_hi", "head_lo"))
        gate_done, par_scaled = lsem("gate_done"), lsem("par_scaled")
        second_read, merged, merged_hi, merged_lo = (lsem(n) for n in ("second_read", "merged", "merged_hi", "merged_lo"))
        x_new, sq_done, sq_sum, xg_hi, xg_lo = (lsem(n) for n in ("x_new", "sq_done", "sq_sum", "xg_hi", "xg_lo"))
        relu_sq, hid_hi, hid_lo, down_scaled = (lsem(n) for n in ("relu_sq", "hid_hi", "hid_lo", "down_scaled"))
        final_gain, final_out = lsem("final_gain"), lsem("final_out")
        layer_range = range(layer_sems[0].num, layer_sems[-1].num + 1)
        assert [s.num for s in layer_sems] == list(layer_range)

        block = ctx.enter_context(nc.Block())

        def unit_done(lay, pos):
            return lay * HALVES + 2 * (pos + 1) + 4

        def head_part(h):
            return (h % 2) * 64

        @block.sync
        def _(sp):
            sp.dma_start(cst[:], consts[:, 0:CKEPT]).then_inc(consts_in, 16)
            sp.dma_start(pos_i, pos_in.broadcast_to([P, SEQ])).then_inc(pos_landed, 16)
            for k in range(KT):
                sp.dma_start(x[:, k], xt[k * P:(k + 1) * P, :]).then_inc(x_in[k], 16)
                if k == 0:
                    sp.dma_start(raw[:, 0], wstream[0]).then_inc(raw_in[0], 16)
            sp.dma_start(raw[:, 1], wstream[1]).then_inc(raw_in[1], 16)
            sp.dma_start(pmat[:, 0, 0:P], consts[:, C_MASK:C_MASK + P]).then_inc(rounding_in, 16)
            sp.dma_start(pmat[0:2 * F_ROW, 1], consts[0:2 * F_ROW, C_SEL:C_SEL + M_HEADS * P]).then_inc(rounding_in, 16)
            with sp.Fori(0, DEPTH * PAIRS // 2 - 1) as n:
                for s in range(2):
                    sp.wait_ge(lo_done, n * 8 + 4 * (s + 1))
                    sp.dma_start(raw[:, s], wstream[2:].rearrange("(n s) p k c -> n s p k c", s=2)[n, s]).then_inc(raw_in[s], 16)
            sp.wait_ge(lo_done, DEPTH * HALVES - 4)
            sp.dma_start(raw[:, 0], wstream[0]).then_inc(raw_in[0], 16)
            for m in range(KT):
                sp.wait_ge(final_out, m + 1)
                sp.dma_start(out[m * P:(m + 1) * P, :], x[:, m, :]).then_inc(stored, 16)
            sp.wait_ge(stored, 16 * KT)

        @block.gpsimd
        def _(pool):
            nc.gpsimd.memset(ones[:], 1.0).then_inc(constants, 1)
            nc.gpsimd.memset(frows[:].bitcast(F32), 0.0).then_inc(constants, 1)
            nc.gpsimd.memset(vn[:, :, :, M_V:M_V + 1], 1.0).then_inc(constants, 1)

            def rest(pairs, base, s):
                for h in range(4):
                    pool.wait_ge(hi_done, pairs + (4 * (base + s) + h + 1))
                    src = raw[:, (base + s) % 2, (h % 2) * 4:(h % 2) * 4 + 4, (h // 2) * P:(h // 2 + 1) * P]
                    nc.gpsimd.tensor_tensor(wlo[:, h], src, whi[:, h].bitcast(F32), ALU.subtract).then_inc(lo_done, 1)

            rest(0, 0, 0)
            for k in range(KT // 2, KT):
                pool.wait_ge(x_in[k], 16)
                nc.gpsimd.tensor_tensor(first_sq[k], x[:, k], x[:, k], ALU.mult).then_inc(pool_squares, 1)
            with pool.Fori(0, DEPTH * PAIRS // 2) as n:
                for s in range(2):
                    rest(n * 8, 1, s)

        @block.scalar
        def _(act):
            steps = [0]

            def link(ins):
                steps[0] += 1
                ins.then_inc(act_step, 1)
                act.wait_ge(act_step, steps[0])

            def split_half(lay, pos, i):
                if isinstance(lay, tuple):
                    l, q = lay
                    act.wait_ge(raw_in[(pos // 2) % 2], l * (8 * PAIRS) + q * (8 * KT) + 16 * (pos // 4 + 1))
                    act.wait_ge(half_used, l * HALVES + q * (4 * KT) + (2 * pos + i + 1))
                else:
                    act.wait_ge(raw_in[(pos // 2) % 2], lay * (8 * PAIRS) + 16 * (pos // 4 + 1))
                    act.wait_ge(half_used, lay * HALVES + (2 * pos + i + 1))
                src = raw[:, (pos // 2) % 2, 4 * i:4 * i + 4, (pos % 2) * P:(pos % 2 + 1) * P]
                nc.scalar.copy(whi[:, (2 * pos + i) % 4], src).then_inc(hi_done, 1)

            def first_round(k):
                act.wait_ge(x_in[k], 16)
                nc.scalar.activation(xg_mix[:, k, 0], x[:, k], ACT.Copy,
                                     scale=cst[:, C_GAIN + k:C_GAIN + k + 1]).then_inc(first_hi, 1)

            act.wait_ge(consts_in, 16)
            first_round(0)
            nc.scalar.activation(first_sq[0], x[:, 0], ACT.Square).then_inc(first_square, 1)
            for i in range(2):
                split_half(0, 0, i)
            for k in range(1, 4):
                first_round(k)
            for i in range(2):
                split_half(0, 1, i)
                first_round(4 + i)
            for k in range(6, KT):
                first_round(k)
            act.wait_ge(angles, 1)
            nc.scalar.activation(sin[:], t1[:], ACT.Sin, scale=cst[:, C_SIGN:C_SIGN + 1]).then_inc(tables, 1)
            nc.scalar.activation(cos[:], t2[:], ACT.Sin, bias=cst[:, C_HALFPI:C_HALFPI + 1], scale=-1.0).then_inc(tables, 1)

            with act.Fori(0, DEPTH) as l:
                steps[0] = 0

                def evacuation(w):
                    kind, j, pos = W_UNITS[w]
                    if kind in ("qk", "gm", "ga", "o", "if"):
                        if kind == "qk":
                            act.wait_ge(conv_out, j + 1)
                            if j:
                                act.wait_ge(qk_done, j)
                            nc.scalar.activation(t3[:], qk[:, j], ACT.Tanh, scale=0.5).then_inc(silu_th, 1)
                            return
                        act.wait_ge(evacuated[bank_of(pos)], bank_uses(pos))
                        if kind == "gm":
                            nc.scalar.activation(th_gate[:, j], za[:, pos % 2], ACT.Tanh, scale=0.5).then_inc(gate_done, 1)
                        elif kind == "ga":
                            nc.scalar.activation(th_gate[:, KT + j], za[:, pos % 2], ACT.Tanh, scale=0.5).then_inc(gate_done, 1)
                        elif kind == "o":
                            if j >= 2:
                                act.wait_ge(head_gated, j - 1)
                            nc.scalar.activation(th_o[:, j % 2], za[:, pos % 2], ACT.Tanh, scale=0.5).then_inc(gate_done, 1)
                        else:
                            act.wait_ge(par_scaled, 1)
                            nc.scalar.activation(rows[:, 1], rows[:, 0], ACT.Tanh, scale=1.0 / CAP,
                                                 bias=small[0:2 * F_ROW, 15, 0:1]).then_inc(gate_th, 1)

                def softplus():
                    act.wait_ge(gate_th, 1)
                    link(nc.scalar.activation(rows[0:M_HEADS, 0], rows[F_ROW:F_ROW + M_HEADS, 1], ACT.Exp, scale=-CAP))
                    nc.scalar.activation(rows[0:M_HEADS, 0], rows[0:M_HEADS, 0], ACT.Ln,
                                         bias=ones[0:M_HEADS, 0:1]).then_inc(gate_sp, 1)

                def att_exponentials(c):
                    nk = CHUNK if c == 0 else 2 * CHUNK
                    act.wait_ge(logits_read, c + 1)
                    if c:
                        act.wait_ge(probs, c)
                    nc.scalar.activation(t1[:, 0:4 * nk], t0[:, 0:4 * nk], ACT.Exp).then_inc(att_exp, 1)
                    act.wait_ge(sink_gap, c + 1)
                    nc.scalar.activation(small[:, 3], small[:, 2], ACT.Exp).then_inc(att_exp, 1)

                def att_copy(c):
                    nk = CHUNK if c == 0 else 2 * CHUNK
                    act.wait_ge(probs_t, c + 1)
                    if c:
                        act.wait_ge(att_o, c)
                    else:
                        act.wait_ge(qk_done, 4)
                    nc.scalar.copy(t3[0:nk], b_pt[0:nk]).then_inc(probs_c, 1)

                def att_round(c):
                    act.wait_ge(att_o, c + 1)
                    nc.scalar.copy(hid[:, 0:4, 0, c * CHUNK:(c + 1) * CHUNK],
                                   b_av[:, 0:256].rearrange("p (a t) -> p a t", a=4)).then_inc(att_hi, 1)

                def mem_decay(h, S):
                    n = SEQ - S * P
                    act.wait_ge(decay_in, 4 * h + S + 1)
                    act.wait_ge(cols_done, 1)
                    if 4 * h + S:
                        act.wait_ge(weights, 4 * h + S)
                    nc.scalar.activation(t2[:, 0:n], b_lg[:, 0:n], ACT.Exp,
                                         bias=bcols[:, 4 * S + h:4 * S + h + 1]).then_inc(decay, 1)

                def round_qk(tiles):
                    act.wait_ge(att_o, NC)
                    for j in tiles:
                        nc.scalar.copy(qk_hi[:, j], qk[:, j]).then_inc(qk_rounded, 1)

                def head_sums(h):
                    for i in range(2):
                        act.wait_ge(summed, 4 * (h + 1))
                        if h:
                            act.wait_ge(head_t, h)
                        nc.scalar.copy(hn[:, 2 * i:2 * i + 2], mem_banks[i][:, 0:2 * (M_V + 1)].rearrange(
                            "p (a d) -> p a d", a=2)).then_inc(sums_out, 1)

                def head_round(h):
                    act.wait_ge(head_gated, h + 1)
                    nc.scalar.activation(hid[:, 4 + h, 0], t0[:], ACT.Copy,
                                         scale=small[:, 14, h:h + 1]).then_inc(head_hi, 1)

                for w, (kind, j, pos) in enumerate(W_UNITS):
                    if w == 3:
                        act.wait_ge(layer_go, l + 1)
                        act.nop(nofuse=True)
                        act.dma_start(par[:], params[l]).then_inc(par_in, 16)
                    if w == 7:
                        for i in range(2):
                            act.wait_ge(vwin_t, i + 1)
                            if i == 0:
                                nc.scalar.copy(vwin[0:CHUNK, 0], b_nm[0:CHUNK, 0:P]).then_inc(act_step, 1)
                                nc.scalar.copy(vwin[:, 1:4], b_nm[:, P:].rearrange("p (a d) -> p a d", a=3)).then_inc(vwin_done, 1)
                                steps[0] += 1
                            else:
                                nc.scalar.copy(vwin[:, 4:8], b_tr[:].rearrange("p (a d) -> p a d", a=4)).then_inc(vwin_done, 1)
                    if 12 <= w < 12 + M_HEADS:
                        h = w - 12
                        act.wait_ge(v_t, h + 1)
                        nc.scalar.copy(vn[:, h, :, 0:M_V], b_tr[:].rearrange("p (s d) -> p s d", s=TB)).then_inc(v_done, 1)
                    c = w - ATT0 - 1
                    if 0 <= c - 1 < NC:
                        att_copy(c - 1)
                    if 0 <= c - 2 < NC:
                        att_round(c - 2)
                    if c == NC:
                        softplus()
                    if NC < c <= NC + 2:
                        round_qk((c - NC - 1, c - NC + 1))
                    h, odd = divmod(w - MEM0, 2)
                    mem = 0 <= h < M_HEADS
                    if odd == 0 and 0 <= h - 1 < M_HEADS:
                        head_sums(h - 1)
                    if mem:
                        mem_decay(h, 2 * odd)
                        split_half(l, pos + 2, 0)
                    if w:
                        evacuation(w - 1)
                    if 0 <= c < NC:
                        att_exponentials(c)
                    if odd == 0 and 0 <= h - 2 < M_HEADS:
                        head_round(h - 2)
                    if mem:
                        mem_decay(h, 2 * odd + 1)
                    else:
                        split_half(l, pos + 2, 0)
                    split_half(l, pos + 2, 1)
                    if pos + 1 == NONE_POS:
                        for i in range(2):
                            split_half(l, pos + 3, i)
                evacuation(len(W_UNITS) - 1)

                for m in range(KT):
                    for i in range(2):
                        split_half(l, BRANCH_POS + m + 2, i)
                    act.wait_ge(merged, m + 1)
                    nc.scalar.activation(xg_mix[:, m, 0], za[:, m % 2], ACT.Copy, scale=0.5).then_inc(merged_hi, 1)

                def new_x(m, n, dst, gcol):
                    if n < KT:
                        act.wait_ge(evacuated[bank_of(OUT_POS + m)], bank_uses(OUT_POS + m))
                    else:
                        act.wait_ge(x_new, m + 1)
                    nc.scalar.activation(dst[:, m, 0], x[:, m], ACT.Copy, scale=par[:, gcol + m:gcol + m + 1]).then_inc(xg_hi, 1)
                    if m < KT - 1:
                        if n:
                            act.wait_ge(sq_sum, n)
                        nc.scalar.activation(sq_t[:], x[:, m], ACT.Square).then_inc(sq_done, 1)

                for m in range(KT):
                    for i in range(2):
                        split_half(l, OUT_POS + m + 2, i)
                    new_x(m, m, xg_mlp, PC_MLP_G)

                def mlp_quarter(q, last):
                    lay = (l, q)
                    for i in range(KT):
                        pos = MLP_POS + i
                        for half in range(2):
                            split_half(lay, pos + 2, half)
                        act.wait_ge(half_used, l * HALVES + q * (4 * KT) + (2 * (pos + 1) + 4))
                        nc.scalar.activation(pmat[:, i % 2], acc[bank_of(pos)][:], ACT.Relu).then_inc(evacuated[bank_of(pos)], 1)
                        act.wait_ge(relu_sq, q * KT + (i + 1))
                        nc.scalar.copy(hid[:, i, 0], za[:, i % 2]).then_inc(hid_hi, 1)
                    for m in range(KT):
                        pos = MLP_POS + KT + m
                        for half in range(2):
                            split_half(lay, pos + 2, half)
                        if last:
                            new_x(m, KT + m, xg_mix, PC_NEXT_G)

                mlp_quarter(0, False)
                with act.Fori(1, QUARTERS - 1) as q:
                    mlp_quarter(q, False)
                mlp_quarter(QUARTERS - 1, True)
                act.drain().then_inc(at_rest, 1)

            act.wait_ge(layer_go, DEPTH + 1)
            for m in range(KT):
                nc.scalar.activation(x[:, m], x[:, m], ACT.Copy,
                                     scale=par[:, PC_NEXT_G + m:PC_NEXT_G + m + 1]).then_inc(final_gain, 1)

        @block.vector
        def _(dve):
            steps = [0]

            def link(ins):
                steps[0] += 1
                ins.then_inc(dve_step, 1)
                dve.wait_ge(dve_step, steps[0])

            def ts(o, a, s1, s2, op0, op1=None):
                return nc.vector.tensor_scalar(o, a, s1, s2, op0, op1) if op1 else nc.vector.tensor_scalar(o, a, s1, s2, op0)

            def stt(o, a, s, b, op0, op1):
                return nc.vector.scalar_tensor_tensor(out=o, in0=a, scalar=s, in1=b, op0=op0, op1=op1)

            def rsqrt(y, v):
                w, t = small[:, 11], small[:, 12]
                link(ts(smalli[:], v.bitcast(I32), 1, None, ALU.logical_shift_right))
                link(ts(y.bitcast(I32), smalli[:], -1.0, float(0x5F3759DF), ALU.mult, ALU.add))
                link(ts(w, v, -0.5, None, ALU.mult))
                for _ in range(3):
                    link(nc.vector.tensor_tensor(t, y, y, ALU.mult))
                    link(nc.vector.tensor_tensor(t, t, w, ALU.mult))
                    link(stt(y, t, 1.5, y, ALU.add, ALU.mult))

            def stat_diagonals(n, squared, summed_up=stat_sum):
                dve.wait_ge(summed_up, n)
                link(ts(small[:, 8], b_ms[:, 0:TB], 1.0 / D_MODEL, EPS, ALU.mult, ALU.add))
                rsqrt(small[:, 9], small[:, 8])
                if squared:
                    link(nc.vector.tensor_tensor(small[:, 9], small[:, 9], small[:, 9], ALU.mult))
                for c in range(TB):
                    ins = ts(ssum[:, c * P:(c + 1) * P], ident, small[:, 9, c:c + 1], None, ALU.mult)
                    ins.then_inc(stat_diag, 1)

            def stat_spread(n):
                dve.wait_ge(stat_bcast, n)
                nc.vector.tensor_copy(invb[:], b_ms[:]).then_inc(stat_done, 1)
                dve.wait_ge(stat_done, n)

            def step(ins):
                steps[0] += 1
                ins.then_inc(setup, 1)
                dve.wait_ge(setup, steps[0])

            def first_rest(k):
                dve.wait_ge(first_hi, k + 1)
                stt(xg_mix[:, k, 1], x[:, k], cst[:, C_GAIN + k:C_GAIN + k + 1], xg_mix[:, k, 0].bitcast(F32),
                    ALU.mult, ALU.subtract).then_inc(mix_lo, 1)

            dve.wait_ge(consts_in, 16)
            dve.wait_ge(pos_landed, 16)
            step(ts(t1[:], pos_i, cst[:, C_FREQ:C_FREQ + 1], None, ALU.mult))
            magic = 12582912.0
            step(ts(t2[:], t1[:], 0.15915494309189535, magic, ALU.mult, ALU.add))
            step(ts(t2[:], t2[:], -magic, None, ALU.add))
            for part in (6.28125, 0.0019340515136718750, 1.2556734959e-06):
                step(stt(t1[:], t2[:], -part, t1[:], ALU.mult, ALU.add))
            step(ts(t1[:], t1[:], 3.1415925, -3.1415925, ALU.min, ALU.max))
            stt(t2[:], t1[:], -1.0, t1[:], ALU.mult, ALU.max).then_inc(angles, 1)
            for k in range(KT):
                first_rest(k)
            dve.wait_ge(first_square, 1)
            for k in range(1, KT):
                if k < KT // 2:
                    step(nc.vector.tensor_tensor(first_sq[k], x[:, k], x[:, k], ALU.mult))
                else:
                    dve.wait_ge(pool_squares, k - KT // 2 + 1)
                step(nc.vector.tensor_tensor(ssum[:], ssum[:], first_sq[k], ALU.add))
            dve.wait_ge(rounding_in, 32)
            step(nc.vector.tensor_copy(ident_r[:], ident))
            step(nc.vector.tensor_copy(mask_r[:], pmat[:, 0, 0:P]))
            step(nc.vector.tensor_copy(sel_r[:], pmat[0:2 * F_ROW, 1].rearrange("p (h m) -> p h m", h=M_HEADS)))
            dve.wait_ge(constants, 3)
            dve.wait_ge(tables, 2)
            dve.wait_ge(mix_lo, KT)
            dve.nop(nofuse=True).then_inc(layer_go, 1)

            def next_layer(n):
                dve.drain()
                dve.wait_ge(at_rest, n)
                dve.nop(nofuse=True)
                dve.sem_clear(layer_range)
                dve.nop(nofuse=True).then_inc(layer_go, 1)

            with dve.Fori(0, DEPTH) as l:
                steps[0] = 0
                dve.wait_ge(layer_go, l + 1)
                dve.nop(nofuse=True)
                link(nc.vector.memset(conv_in[:, 0:TAPS - 1], 0.0))

                def evacuation(w):
                    kind, j, pos = W_UNITS[w]
                    src, done = acc[bank_of(pos)], evacuated[bank_of(pos)]
                    if kind == "qk" and j:
                        dve.wait_ge(conv_out, j)
                    if kind == "qa":
                        dst, sc = qa[:, j], invb[:]
                    elif kind == "qk":
                        dst, sc = conv_in[:, TAPS - 1:], invb[:]
                    elif kind == "if":
                        dst, sc, src = rows[:, 0], invb[0:2 * F_ROW], acc[bank_of(pos)][0:2 * F_ROW]
                    else:
                        dst, sc = za[:, pos % 2], invb[:]
                        if kind in ("gm", "ga", "o"):
                            earlier = [k for k, _, _ in W_UNITS[:w]]
                            n = sum(k in ("gm", "ga", "o") for k in earlier) - 1
                            if n >= 1:
                                dve.wait_ge(gate_done, n)
                            else:
                                dve.wait_ge(v_t, M_HEADS)
                        elif kind == "vm":
                            if j == 0:
                                dve.wait_ge(vwin_t, 2)
                                dve.wait_ge(roped, 5)
                            elif j >= 2:
                                dve.wait_ge(v_t, j - 1)
                    dve.wait_ge(half_used, unit_done(l, pos))
                    nc.vector.tensor_tensor(dst, src[:] if kind != "if" else src, sc, ALU.mult).then_inc(done, 1)
                    if kind == "qk":
                        dve.wait_ge(done, bank_uses(pos))
                        link(ts(qk[:, j], conv_in[:, 0:SEQ], par[:, PC_CONV + 4 * j:PC_CONV + 4 * j + 1], None, ALU.mult))
                        for t in range(1, TAPS):
                            col = PC_CONV + 4 * j + t
                            ins = stt(qk[:, j], conv_in[:, t:t + SEQ], par[:, col:col + 1], qk[:, j], ALU.mult, ALU.add)
                            if t < TAPS - 1:
                                link(ins)
                            else:
                                ins.then_inc(conv_out, 1)

                def silu(j):
                    dve.wait_ge(silu_th, j + 1)
                    stt(qk[:, j], t3[:], 1.0, qk[:, j], ALU.add, ALU.mult).then_inc(qk_done, 1)

                def rope(n):
                    j = ROPE_ORDER[n]
                    src = qa[:, j] if j < 4 else za[:, 0]
                    dve.wait_ge(evacuated[bank_of(j)], bank_uses(j))
                    link(nc.vector.stream_shuffle(t1[:], src, PARTNER))
                    link(nc.vector.tensor_tensor(t1[:], t1[:], sin[:], ALU.mult))
                    link(nc.vector.tensor_tensor(src, src, cos[:], ALU.mult))
                    if j < 4:
                        nc.vector.tensor_tensor(src, src, t1[:], ALU.add).then_inc(roped, 1)
                    else:
                        for g in range(A_KV):
                            s = slice(64 * g, 64 * g + 64)
                            for e in range(2):
                                ins = nc.vector.tensor_tensor(kd[64 * e:64 * e + 64, g], za[s, 0], t1[s], ALU.add)
                                if g and e:
                                    ins.then_inc(roped, 1)
                                else:
                                    link(ins)
                    dve.wait_ge(roped, n + 1)

                def decay_rows():
                    dve.wait_ge(gate_sp, 1)
                    for S in range(TB):
                        link(nc.vector.tensor_tensor_scan(frow[:, SEG[S]:SEG[S + 1]], ones[0:M_HEADS, S * P:],
                                                          rows[0:M_HEADS, 0, S * P:], 0.0, ALU.mult, ALU.subtract))

                def gate_rows():
                    for S in range(TB):
                        blk = slice(S * P, (S + 1) * P)
                        link(stt(rows[0:M_HEADS, 0, blk], rows[0:M_HEADS, 1, blk], CAP, frow[:, SEG[S]:SEG[S] + P],
                                 ALU.mult, ALU.subtract))
                    link(nc.vector.tensor_copy(frows[0:M_HEADS], frow[:]))
                    nc.vector.tensor_tensor(frows[F_ROW:F_ROW + M_HEADS], frow[:], frows[0:M_HEADS].bitcast(F32),
                                            ALU.subtract).then_inc(rows_done, 1)
                    dve.wait_ge(rows_done, 1)

                def qk_rest(tiles, n):
                    for i, j in enumerate(tiles):
                        dve.wait_ge(qk_rounded, n + i + 1)
                        nc.vector.tensor_tensor(qk_lo[:, j], qk[:, j], qk_hi[:, j].bitcast(F32),
                                                ALU.subtract).then_inc(qk_split, 1)

                def gate_cols():
                    dve.wait_ge(cols_t, 1)
                    nc.vector.tensor_copy(bcols[:], b_tr[:, 0:TB * M_HEADS]).then_inc(cols_done, 1)
                    dve.wait_ge(cols_done, 1)

                def att_softmax(c):
                    nk = CHUNK if c == 0 else 2 * CHUNK
                    lg = b_lg[:, 0:4 * nk].rearrange("p (a k) -> p a k", a=4)
                    tv = t0[:, 0:4 * nk].rearrange("p (a k) -> p a k", a=4)
                    ev = t1[:, 0:4 * nk].rearrange("p (a k) -> p a k", a=4)
                    sink = par[:, PC_SINK:PC_SINK + 4]
                    dve.wait_ge(logits, c + 1)
                    link(nc.vector.tensor_reduce(small[:, 0], lg, AX.X, ALU.max))
                    link(stt(small[:, 1], small[:, 0], 0.125, sink, ALU.mult, ALU.max))
                    stt(tv, lg, 0.125, small[:, 1].unsqueeze(2).broadcast_to([P, 4, nk]),
                        ALU.mult, ALU.subtract).then_inc(logits_read, 1)
                    nc.vector.tensor_tensor(small[:, 2], sink, small[:, 1], ALU.subtract).then_inc(sink_gap, 1)
                    dve.wait_ge(att_exp, 2 * c + 2)
                    link(nc.vector.tensor_reduce(small[:, 4], ev, AX.X, ALU.add))
                    link(nc.vector.tensor_tensor(small[:, 4], small[:, 4], small[:, 3], ALU.add))
                    link(nc.vector.reciprocal(small[:, 5], small[:, 4]))
                    if c:
                        dve.wait_ge(probs_t, c)
                    nc.vector.tensor_tensor(pmat[:, 0, 0:4 * nk].rearrange("p (a k) -> p a k", a=4), ev,
                                            small[:, 5].unsqueeze(2).broadcast_to([P, 4, nk]), ALU.mult).then_inc(probs, 1)
                    dve.wait_ge(probs, c + 1)

                def att_rest(c):
                    dve.wait_ge(att_hi, c + 1)
                    dst = hid[:, 0:4, :, c * CHUNK:(c + 1) * CHUNK]
                    nc.vector.tensor_tensor(dst[:, :, 1], b_av[:, 0:256].rearrange("p (a t) -> p a t", a=4),
                                            dst[:, :, 0].bitcast(F32), ALU.subtract).then_inc(att_lo, 1)

                def mem_weights(h, S):
                    n = SEQ - S * P
                    i = 4 * h + S
                    dve.wait_ge(scores_in, i + 1)
                    dve.wait_ge(decay, i + 1)
                    if i >= 2:
                        dve.wait_ge(summed, i - 1)
                    if i < 2:
                        dve.wait_ge(probs_t, NC)
                    stt(pmat[:, i % 2, 0:n], b_pt[:, 0:n], 0.25 * M_QK ** -0.5, t2[:, 0:n], ALU.mult, ALU.mult).then_inc(weights, 1)

                den, rd, ms = small[:, 4], small[:, 5], small[:, 6]
                num = hn[:, :, 0:M_V]

                def head_squares(h):
                    dve.wait_ge(sums_out, 2 * h + 2)
                    link(stt(den, hn[:, :, M_V], -1.0, hn[:, :, M_V], ALU.mult, ALU.max))
                    link(ts(den, den, 1.0, None, ALU.max))
                    link(nc.vector.reciprocal(rd, den))
                    tv = t1[:].rearrange("p (a d) -> p a d", a=TB)
                    link(nc.vector.tensor_tensor(tv, num, num, ALU.mult))
                    link(nc.vector.tensor_reduce(ms, tv, AX.X, ALU.add))
                    link(nc.vector.tensor_tensor(ms, ms, rd, ALU.mult))
                    link(nc.vector.tensor_tensor(ms, ms, rd, ALU.mult))
                    link(ts(ms, ms, 1.0 / M_V, EPS, ALU.mult, ALU.add))

                def head_normalise(h):
                    rsqrt(small[:, 7], ms)
                    link(nc.vector.tensor_tensor(rd, rd, small[:, 7], ALU.mult))
                    nc.vector.tensor_tensor(num, num, rd.unsqueeze(2).broadcast_to([P, TB, M_V]), ALU.mult).then_inc(head_norm, 1)
                    dve.wait_ge(head_norm, h + 1)

                def head_gate(h):
                    dve.wait_ge(head_t, h + 1)
                    scalar_kinds = [(k, jj) for k, jj, _ in W_UNITS if k in ("gm", "ga", "o")]
                    dve.wait_ge(gate_done, scalar_kinds.index(("o", h)) + 1)
                    stt(t0[:], th_o[:, h % 2], 1.0, b_tr[:], ALU.add, ALU.mult).then_inc(head_gated, 1)

                def head_rest(h):
                    dve.wait_ge(head_hi, h + 1)
                    stt(hid[:, 4 + h, 1], t0[:], small[:, 14, h:h + 1], hid[:, 4 + h, 0].bitcast(F32),
                        ALU.mult, ALU.subtract).then_inc(head_lo, 1)
                    dve.wait_ge(head_lo, h + 1)

                for w, (kind, j, pos) in enumerate(W_UNITS):
                    if w == 3:
                        stat_diagonals(1, False)
                        stat_spread(1)
                        for u in range(2):
                            evacuation(u)
                    if w == 5:
                        dve.wait_ge(par_in, l * 16 + 16)
                        link(ts(small[:, 14], par[:, PC_HEAD_G:PC_HEAD_G + 4], 0.5, None, ALU.mult))
                        ts(small[0:2 * F_ROW, 15, 0:1], par[0:2 * F_ROW, PC_GATE_B:PC_GATE_B + 1], 1.0 / CAP, None,
                           ALU.mult).then_inc(par_scaled, 1)
                    h, odd = divmod(w - MEM0, 2)
                    mem = 0 <= h < M_HEADS
                    if mem:
                        mem_weights(h, 2 * odd)
                    if w >= 3:
                        evacuation(w - 1)
                    for n in ROPE_SLOT.get(w, []):
                        rope(n)
                    if w >= 8 and W_UNITS[w - 2][0] == "qk":
                        silu(W_UNITS[w - 2][1])
                    c = w - ATT0 - 1
                    if 0 <= c - 2 < NC:
                        att_rest(c - 2)
                    if 0 <= c < NC:
                        att_softmax(c)
                    if c == NC:
                        decay_rows()
                    if c == NC + 1:
                        gate_rows()
                    if c == NC + 2:
                        gate_cols()
                    if NC < c <= NC + 2:
                        qk_rest((c - NC - 1, c - NC + 1), 2 * (c - NC - 1))
                    if odd == 0 and 0 <= h - 2 < M_HEADS:
                        head_gate(h - 2)
                    if odd == 0 and 0 <= h - 1 < M_HEADS:
                        head_squares(h - 1)
                    if mem:
                        mem_weights(h, 2 * odd + 1)
                    if odd == 0 and 0 <= h - 2 < M_HEADS:
                        head_rest(h - 2)
                    if odd == 0 and 0 <= h - 1 < M_HEADS:
                        head_normalise(h - 1)
                evacuation(len(W_UNITS) - 1)
                n_gates = sum(u[0] in ("gm", "ga", "o") for u in W_UNITS)

                for m in range(KT):
                    pos = BRANCH_POS + m
                    z = za[:, m % 2]
                    dve.wait_ge(gate_done, n_gates)
                    dve.wait_ge(half_used, unit_done(l, pos))
                    stt(z, th_gate[:, KT + m], 1.0, acc[bank_of(pos)][:], ALU.add, ALU.mult).then_inc(evacuated[bank_of(pos)], 1)
                    stt(t0[:], th_gate[:, m], 1.0, branch_banks[m % 2][:], ALU.add, ALU.mult).then_inc(second_read, 1)
                    dve.wait_ge(second_read, m + 1)
                    nc.vector.tensor_tensor(z, z, t0[:], ALU.add).then_inc(merged, 1)
                    dve.wait_ge(merged_hi, m + 1)
                    stt(xg_mix[:, m, 1], z, 0.5, xg_mix[:, m, 0].bitcast(F32), ALU.mult, ALU.subtract).then_inc(merged_lo, 1)

                def new_x(m, n, dst, gcol, rounded):
                    if m == KT - 1:
                        nc.vector.tensor_tensor(sq_t[:], x[:, m], x[:, m], ALU.mult).then_inc(sq_done, 1)
                    dve.wait_ge(xg_hi, n + 1)
                    stt(dst[:, m, 1], x[:, m], par[:, gcol + m:gcol + m + 1], dst[:, m, 0].bitcast(F32),
                        ALU.mult, ALU.subtract).then_inc(rounded, 1)
                    dve.wait_ge(sq_done, n + 1)
                    if m == 0:
                        nc.vector.tensor_copy(ssum[:], sq_t[:]).then_inc(sq_sum, 1)
                    else:
                        nc.vector.tensor_tensor(ssum[:], ssum[:], sq_t[:], ALU.add).then_inc(sq_sum, 1)
                    dve.wait_ge(sq_sum, n + 1)
                    if n == 2 * KT - 1:
                        dve.nop(nofuse=True).then_inc(final_squares, 1)

                for m in range(KT):
                    pos = OUT_POS + m
                    dve.wait_ge(half_used, unit_done(l, pos))
                    nc.vector.tensor_tensor(x[:, m], x[:, m], acc[bank_of(pos)][:], ALU.add).then_inc(evacuated[bank_of(pos)], 1)
                    dve.wait_ge(evacuated[bank_of(pos)], bank_uses(pos))
                    new_x(m, m, xg_mlp, PC_MLP_G, xg_lo)

                def mlp_quarter(q, first, last):
                    for i in range(KT):
                        pos = MLP_POS + i
                        if first and i == 2:
                            stat_diagonals(2, True)
                        if first and i == 4:
                            stat_spread(2)
                        dve.wait_ge(evacuated[bank_of(pos)], q * KT + bank_uses(pos))
                        if i >= 2:
                            dve.wait_ge(hid_lo, q * KT + (i - 1))
                        nc.vector.tensor_tensor(za[:, i % 2], pmat[:, i % 2], pmat[:, i % 2], ALU.mult).then_inc(relu_sq, 1)
                        dve.wait_ge(hid_hi, q * KT + (i + 1))
                        nc.vector.tensor_tensor(hid[:, i, 1], za[:, i % 2], hid[:, i, 0].bitcast(F32), ALU.subtract).then_inc(hid_lo, 1)
                        if i == KT - 1:
                            dve.wait_ge(hid_lo, q * KT + KT)
                    for m in range(KT):
                        pos = MLP_POS + KT + m
                        dve.wait_ge(half_used, l * HALVES + q * (4 * KT) + (2 * (pos + 1) + 4))
                        nc.vector.tensor_tensor(t0[:], acc[bank_of(pos)][:], invb[:], ALU.mult).then_inc(evacuated[bank_of(pos)], 1)
                        dve.wait_ge(evacuated[bank_of(pos)], q * KT + bank_uses(pos))
                        nc.vector.tensor_tensor(x[:, m], x[:, m], t0[:], ALU.add).then_inc(x_new if last else down_scaled, 1)
                        if last:
                            dve.wait_ge(x_new, m + 1)
                            new_x(m, KT + m, xg_mix, PC_NEXT_G, mix_lo)
                        else:
                            dve.wait_ge(down_scaled, q * KT + (m + 1))

                mlp_quarter(0, True, False)
                with dve.Fori(1, QUARTERS - 1) as q:
                    mlp_quarter(q, False, False)
                mlp_quarter(QUARTERS - 1, False, True)
                next_layer(2 * l + 2)

            steps[0] = 0
            stat_diagonals(1, False, final_sum)
            dve.wait_ge(stat_bcast, 1)
            for m in range(KT):
                dve.wait_ge(final_gain, m + 1)
                nc.vector.tensor_tensor(x[:, m], x[:, m], b_ms[:], ALU.mult).then_inc(final_out, 1)

        @block.tensor
        def _(pe):
            pe.sem_inc(half_used, 4)

            def stat_sums(done):
                for c in range(TB):
                    last = nc.tensor.matmul(b_ms[:, c:c + 1], ssum[:, c * P:(c + 1) * P], ones[:, 0:1], start=True, stop=True)
                last.then_inc(done, 1)

            def stat_rows(n):
                for c in range(TB):
                    pe.wait_ge(stat_diag, TB * (n - 1) + c + 1)
                    last = nc.tensor.matmul(b_ms[:, c * P:(c + 1) * P], ones[:, 0:P], ssum[:, c * P:(c + 1) * P],
                                            start=True, stop=True)
                last.then_inc(stat_bcast, 1)

            with pe.Fori(0, DEPTH) as l:
                def unit_start(pos):
                    if bank_uses(pos) > 1:
                        pe.wait_ge(evacuated[bank_of(pos)], bank_uses(pos) - 1)

                def unit_half(pos, i, rhs, ready=None, base=0, bank=None, whole=True):
                    pe.wait_ge(lo_done, l * HALVES + (2 * pos + i + 1))
                    s = (2 * pos + i) % 4
                    b = acc[bank_of(pos)] if bank is None else bank
                    for k in range(4):
                        kk = 4 * i + k
                        if ready is not None:
                            pe.wait_ge(ready, base + (kk + 1))
                        for q, (wt, a) in enumerate(((whi, 0), (whi, 1), (wlo, 0))):
                            last = nc.tensor.matmul(b[:], wt[:, s, k], rhs[:, kk, a],
                                                    start=(k == 0 and q == 0 and (i == 0 or not whole)),
                                                    stop=(k == 3 and q == 2 and (i == 1 or not whole)))
                    last.then_inc(half_used, 1)

                def value_windows():
                    pos = W_UNITS[5][2]
                    pe.wait_ge(evacuated[bank_of(pos)], bank_uses(pos))
                    v = za[:, 1]
                    nc.tensor.transpose(b_nm[0:CHUNK, 0:P], v[:, 0:CHUNK], ident)
                    for c in range(1, NC):
                        bank = b_nm if c < 4 else b_tr
                        last = nc.tensor.transpose(bank[:, (c % 4) * P:(c % 4 + 1) * P], v[:, (c - 1) * CHUNK:(c + 1) * CHUNK], ident)
                        if c % 4 == 3:
                            last.then_inc(vwin_t, 1)

                def turn_values(h):
                    pos = W_UNITS[10 + h][2]
                    pe.wait_ge(evacuated[bank_of(pos)], bank_uses(pos))
                    if h == 0:
                        pe.wait_ge(vwin_done, 2)
                    else:
                        pe.wait_ge(v_done, h)
                    for S in range(TB):
                        last = nc.tensor.transpose(b_tr[:, S * P:(S + 1) * P], za[:, pos % 2, S * P:(S + 1) * P], ident)
                    last.then_inc(v_t, 1)

                def turn_columns():
                    pe.wait_ge(rows_done, 1)
                    pe.wait_ge(v_done, M_HEADS)
                    for S in range(TB):
                        last = nc.tensor.transpose(b_tr[:, S * M_HEADS:(S + 1) * M_HEADS], rows[0:M_HEADS, 0, S * P:(S + 1) * P],
                                                   cst[0:M_HEADS, C_ID:C_ID + M_HEADS])
                    last.then_inc(cols_t, 1)

                def att_logits(c):
                    nk = CHUNK if c == 0 else 2 * CHUNK
                    k0 = max(c - 1, 0) * CHUNK
                    if c == 0:
                        pe.wait_ge(roped, 5)
                    else:
                        pe.wait_ge(logits_read, c)
                    for a in range(PAIRS_H):
                        for e in range(2):
                            s = slice(64 * e, 64 * e + 64)
                            last = nc.tensor.matmul(b_lg[s, a * nk:(a + 1) * nk], qa[s, a, c * CHUNK:(c + 1) * CHUNK],
                                                    kd[s, a // 2, k0:k0 + nk], start=True, stop=True)
                    last.then_inc(logits, 1)

                def att_turn(c):
                    nk = CHUNK if c == 0 else 2 * CHUNK
                    pe.wait_ge(probs, c + 1)
                    if c:
                        pe.wait_ge(probs_c, c)
                    for a in range(PAIRS_H):
                        last = nc.tensor.transpose(b_pt[0:nk, a * P:(a + 1) * P], pmat[:, 0, a * nk:(a + 1) * nk], ident)
                    last.then_inc(probs_t, 1)

                def att_values(c):
                    nk = CHUNK if c == 0 else 2 * CHUNK
                    pe.wait_ge(probs_c, c + 1)
                    if c == 0:
                        pe.wait_ge(vwin_done, 2)
                    else:
                        pe.wait_ge(att_lo, c)
                    pv = t3[0:nk].rearrange("p (a e t) -> p a e t", a=PAIRS_H, e=2)
                    for g in range(A_KV):
                        for e in range(2):
                            last = nc.tensor.matmul(b_av[64 * e:64 * e + 64, g * 2 * CHUNK:(g + 1) * 2 * CHUNK],
                                                    vwin[0:nk, c, g * A_DIM:(g + 1) * A_DIM], pv[:, 2 * g:2 * g + 2, e],
                                                    start=True, stop=True)
                    last.then_inc(att_o, 1)

                def mem_inputs(h, S):
                    i = 4 * h + S
                    n = SEQ - S * P
                    if i == 0:
                        pe.wait_ge(rows_done, 1)
                        pe.wait_ge(logits_read, NC)
                        pe.wait_ge(probs_c, NC)
                        pe.wait_ge(qk_split, 4)
                    else:
                        pe.wait_ge(decay, i)
                    nc.tensor.matmul(b_lg[:, 0:n], sel_r[:, h], frows[:, SEG[S]:SEG[S + 1]], start=True, stop=True,
                                 skip_group_check=True)
                    nc.tensor.matmul(b_lg[:, 0:P], ident_r[:], mask_r[:], start=False, stop=True,
                                     skip_group_check=True).then_inc(decay_in, 1)
                    if i:
                        pe.wait_ge(weights, i)
                    s = slice(head_part(h), head_part(h) + M_QK)
                    k = [t[s, 2 + h // 2, S * P:(S + 1) * P] for t in (qk_hi, qk_lo)]
                    q = [t[s, h // 2, S * P:SEQ] for t in (qk_hi, qk_lo)]
                    for a, b in ((0, 0), (0, 1), (1, 0)):
                        last = nc.tensor.matmul(b_pt[:, 0:n], k[a], q[b], start=(a + b == 0), stop=(a == 1))
                    last.then_inc(scores_in, 1)

                def mem_sums(h, S):
                    i = 4 * h + S
                    pe.wait_ge(weights, i + 1)
                    if S == 0 and h:
                        pe.wait_ge(sums_out, 2 * h)
                    if i == 0:
                        pe.wait_ge(vwin_done, 2)
                    for T in range(S, TB):
                        bank = mem_banks[T // 2]
                        last = nc.tensor.matmul(bank[:, (T % 2) * (M_V + 1):(T % 2 + 1) * (M_V + 1)],
                                                pmat[:, i % 2, (T - S) * P:(T - S + 1) * P], vn[:, h, S, :],
                                                start=(S == 0 and T % 2 == 0), stop=(S == T), skip_group_check=True)
                    last.then_inc(summed, 1)

                def turn_head(h):
                    pe.wait_ge(head_norm, h + 1)
                    if h:
                        pe.wait_ge(head_gated, h)
                    else:
                        pe.wait_ge(cols_done, 1)
                    for T in range(TB):
                        last = nc.tensor.transpose(b_tr[:, T * P:(T + 1) * P], hn[:, T, 0:M_V], ident)
                    last.then_inc(head_t, 1)

                for w, (kind, j, pos) in enumerate(W_UNITS):
                    h, odd = divmod(w - MEM0, 2)
                    mem = 0 <= h < M_HEADS
                    if mem:
                        mem_inputs(h, 2 * odd)
                    unit_start(pos)
                    rounded, base = (mix_lo, l * KT) if w == 0 else (None, 0)
                    unit_half(pos, 0, xg_mix, rounded, base)
                    if mem:
                        mem_sums(h, 2 * odd)
                        mem_inputs(h, 2 * odd + 1)
                    if w == 2:
                        pe.wait_ge(layer_go, l + 1)
                        stat_sums(stat_sum)
                    if w == 3:
                        stat_rows(1)
                    unit_half(pos, 1, xg_mix, rounded, base)
                    if mem:
                        mem_sums(h, 2 * odd + 1)
                    if pos + 1 == NONE_POS:
                        pe.wait_ge(lo_done, l * HALVES + 2 * (NONE_POS + 1))
                        pe.nop(nofuse=True)
                        pe.drain().then_inc(half_used, 2)
                    if w == 6:
                        value_windows()
                    if 11 <= w < 11 + M_HEADS:
                        turn_values(w - 11)
                    if w == MEM0 - 2:
                        turn_columns()
                    c = w - ATT0
                    if 0 <= c - 2 < NC:
                        att_values(c - 2)
                    if 0 <= c - 1 < NC:
                        att_turn(c - 1)
                    if 0 <= c < NC:
                        att_logits(c)
                    if 0 <= h - 1 < M_HEADS and odd == 1:
                        turn_head(h - 1)

                for m in range(KT):
                    pos = BRANCH_POS + m
                    unit_start(pos)
                    if m == 0:
                        pe.wait_ge(att_lo, NC)
                    unit_half(pos, 0, hid, whole=False)
                    if m == 0:
                        pe.wait_ge(head_lo, M_HEADS)
                    if m >= 2:
                        pe.wait_ge(second_read, m - 1)
                    unit_half(pos, 1, hid, bank=branch_banks[m % 2], whole=False)

                for m in range(KT):
                    pos = OUT_POS + m
                    unit_start(pos)
                    for i in range(2):
                        unit_half(pos, i, xg_mix, ready=merged_lo if m == 0 else None)

                def mlp_unit(q, pos, rhs, ready, base):
                    pe.wait_ge(evacuated[bank_of(pos)], q * KT + (bank_uses(pos) - 1))
                    for i in range(2):
                        pe.wait_ge(lo_done, l * HALVES + q * (4 * KT) + (2 * pos + i + 1))
                        s = (2 * pos + i) % 4
                        for k in range(4):
                            kk = 4 * i + k
                            if ready is not None:
                                pe.wait_ge(ready, base + (kk + 1))
                            for t, (wt, a) in enumerate(((whi, 0), (whi, 1), (wlo, 0))):
                                last = nc.tensor.matmul(acc[bank_of(pos)][:], wt[:, s, k], rhs[:, kk, a],
                                                        start=(kk == 0 and t == 0), stop=(kk == KT - 1 and t == 2))
                        last.then_inc(half_used, 1)

                def mlp_quarter(q, first):
                    for i in range(KT):
                        mlp_unit(q, MLP_POS + i, xg_mlp, xg_lo if first and i == 0 else None, 0)
                        if first and i == 1:
                            pe.wait_ge(sq_sum, KT)
                            stat_sums(stat_sum)
                        if first and i == 3:
                            stat_rows(2)
                    for m in range(KT):
                        mlp_unit(q, MLP_POS + KT + m, hid, hid_lo if m == 0 else None, q * KT)

                mlp_quarter(0, True)
                with pe.Fori(1, QUARTERS - 1) as q:
                    mlp_quarter(q, False)
                mlp_quarter(QUARTERS - 1, False)
                pe.wait_ge(evacuated[0], (QUARTERS - 1) * KT + bank_uses(MLP_POS + 2 * KT - 2))
                pe.drain().then_inc(at_rest, 1)

            pe.wait_ge(final_squares, DEPTH)
            stat_sums(final_sum)
            pe.wait_ge(layer_go, DEPTH + 1)
            pe.nop(nofuse=True)
            stat_rows(1)


_OUT = (D_MODEL, SEQ)


def kernel(**inputs):
    import numpy as np
    import concourse.bacc as bacc
    from concourse import mybir as mb
    from concourse.bass_utils import run_bass_kernel_spmd

    a = {n: np.asarray(v) for n, v in inputs.items()}

    cst = np.zeros((P, CCOLS), np.float32)
    cst[:, C_ID:C_ID + P] = np.eye(P)
    cst[:, C_MASK:C_MASK + P] = np.tril(np.full((P, P), MASKED), -1)
    half = ROT_DIM // 2
    cst[:, C_SIGN] = 1.0
    for head in range(2):
        for i in range(half):
            lo, hi = head * A_DIM + i, head * A_DIM + half + i
            cst[lo, C_SIGN] = -1.0
            cst[[lo, hi], C_FREQ] = np.float32(ROPE_THETA) ** np.float32(-2 * i / ROT_DIM)
    for h in range(M_HEADS):
        cst[[h, F_ROW + h], C_SEL + h * P:C_SEL + (h + 1) * P] = 1.0
    cst[:, C_HALFPI] = np.pi / 2
    cst[:, C_GAIN:C_GAIN + KT] = a["norm_mix_g"][0].reshape(KT, P).T

    w_in = a["w_in"]
    widths = (("qk", 4 * P), ("vm", 4 * P), ("if", 2 * M_HEADS), ("o", 4 * P), ("qa", 4 * P), ("ka", P), ("va", P),
              ("gm", 8 * P), ("ga", 8 * P))
    first, at = {}, 0
    for kind, width in widths:
        first[kind] = at
        at += width
    stream = np.zeros((DEPTH, PAIRS, P, KT, 2, P), np.float32)

    def put(lay, pos, w):
        stream[lay, pos // 2, :, :, pos % 2, :] = w.reshape(KT, P, P).transpose(1, 0, 2)

    for lay in range(DEPTH):
        for kind, j, pos in W_UNITS:
            if kind == "if":
                gates = np.zeros((D_MODEL, P), np.float32)
                c = first["if"]
                gates[:, 0:M_HEADS] = w_in[lay][:, c:c + M_HEADS]
                gates[:, F_ROW:F_ROW + M_HEADS] = w_in[lay][:, c + M_HEADS:c + 2 * M_HEADS]
                put(lay, pos, gates)
            else:
                c = first[kind] + j * P
                put(lay, pos, w_in[lay][:, c:c + P])
        both = np.concatenate([a["w_branch_a"][lay], a["w_branch_m"][lay]], axis=0)
        for m in range(KT):
            cols = slice(m * P, (m + 1) * P)
            put(lay, BRANCH_POS + m, both[:, cols])
            put(lay, OUT_POS + m, a["w_out"][lay][:, cols])
        for q in range(QUARTERS):
            for m in range(KT):
                c = (q * KT + m) * P
                put(lay, MLP_POS + 2 * KT * q + m, a["w_up"][lay][:, c:c + P])
                put(lay, MLP_POS + 2 * KT * q + KT + m,
                    a["w_down"][lay][q * D_MODEL:(q + 1) * D_MODEL, m * P:(m + 1) * P])

    gains = np.concatenate([a["norm_mix_g"][1:], a["final_norm_g"][None]], axis=0)
    par = np.zeros((DEPTH, P, PCOLS), np.float32)
    for lay in range(DEPTH):
        par[lay, :, PC_CONV:PC_CONV + 16] = a["conv_qk_w"][lay].T.reshape(4, P, TAPS).transpose(1, 0, 2).reshape(P, 16)
        par[lay, :, PC_MLP_G:PC_MLP_G + KT] = a["norm_mlp_g"][lay].reshape(KT, P).T
        par[lay, :, PC_NEXT_G:PC_NEXT_G + KT] = gains[lay].reshape(KT, P).T
        par[lay, :, PC_HEAD_G:PC_HEAD_G + 4] = a["mlstm_norm_g"][lay].reshape(4, P).T
        par[lay, 0:M_HEADS, PC_GATE_B] = a["mlstm_gate_b"][lay][:M_HEADS]
        par[lay, F_ROW:F_ROW + M_HEADS, PC_GATE_B] = a["mlstm_gate_b"][lay][M_HEADS:]
        par[lay, :, PC_SINK:PC_SINK + 4] = np.repeat(a["attn_sinks"][lay].reshape(4, 2).T, CHUNK, axis=0)

    arrays = {
        "x_t": np.ascontiguousarray(a["x"][0].T),
        "positions": np.ascontiguousarray(a["positions"]),
        "consts": cst,
        "params": par,
        "w_stream": stream.reshape(DEPTH * PAIRS, P, KT, 2 * P),
    }
    nc = bacc.Bacc("TRN2", target_bir_lowering=False, num_devices=1)
    args = [nc.dram_tensor(n, v.shape, mb.dt.from_np(v.dtype), kind="ExternalInput").ap() for n, v in arrays.items()]
    out = nc.dram_tensor("y_t", _OUT, mb.dt.float32, kind="ExternalOutput").ap()
    program(nc, *args, out)
    r = run_bass_kernel_spmd(nc, [arrays], core_ids=[0])
    return np.ascontiguousarray(r.results[0]["y_t"].T)[None]
```
